# Optimizing a Trainium2 kernel written in Bass

```python
import math
import jax
import jax.numpy as jnp
from jax import lax
import numpy as np
import jax, jax.numpy as jnp

D_MODEL = 2048
BATCH = 1
SEQ = 256
DEPTH = 2

N_A_LAYERS = DEPTH // 2
N_B_LAYERS = DEPTH - N_A_LAYERS

SSM_WIDTH = D_MODEL // 2
SSM_GROUP = 16
SSM_GROUPS = SSM_WIDTH // SSM_GROUP
SSM_STATE = 64
DT_MIN = 0.001
DT_MAX = 0.1

N_HEADS = 16
HEAD_DIM = 128
N_KV_HEADS = 4
HEADS_PER_KV = N_HEADS // N_KV_HEADS
ATTN_WIDTH = N_HEADS * HEAD_DIM
KV_WIDTH = N_KV_HEADS * HEAD_DIM
N_BRANCH = 3
CMP_BLOCK = 32
CMP_STRIDE = 16
SEL_BLOCK = 64
N_SELECT = 16
WINDOW = 512
Q_BLOCK = 64
B_IN_WIDTH = ATTN_WIDTH * (1 + N_BRANCH) + N_BRANCH * N_HEADS

LN_EPS = 1e-5
DEEPNORM_ALPHA = (2 * DEPTH) ** 0.25
DEEPNORM_BETA = (8 * DEPTH) ** -0.25
MASK_VALUE = -1e30
FORCE_SCORE = 1e6


def layer_norm(x, g, b):
    x32 = x.astype(jnp.float32)
    mu = jnp.mean(x32, axis=-1, keepdims=True)
    var = jnp.mean(jnp.square(x32 - mu), axis=-1, keepdims=True)
    return ((x32 - mu) * lax.rsqrt(var + LN_EPS) * g.astype(jnp.float32) + b.astype(jnp.float32)).astype(x.dtype)

def _complex_linear_combine(e1, e2):
    a1r, a1i, b1r, b1i = e1
    a2r, a2i, b2r, b2i = e2
    return (a2r * a1r - a2i * a1i,
            a2r * a1i + a2i * a1r,
            a2r * b1r - a2i * b1i + b2r,
            a2r * b1i + a2i * b1r + b2i)

def s5_mixer(x, w_in, lam_re, lam_im, log_dt, b_re, b_im, c_re, c_im, d_skip, w_glu, b_glu, w_out):
    bsz, seq, _ = x.shape
    f32 = jnp.float32
    u, z = jnp.split(x @ w_in, 2, axis=-1)
    lr = lam_re.astype(f32)
    li = lam_im.astype(f32)
    dt = jnp.exp(log_dt.astype(f32))[:, None]
    mag = jnp.exp(lr * dt)
    ar = mag * jnp.cos(li * dt)
    ai = mag * jnp.sin(li * dt)
    inv_abs2 = 1.0 / (lr * lr + li * li)
    cr = ((ar - 1.0) * lr + ai * li) * inv_abs2
    ci = (ai * lr - (ar - 1.0) * li) * inv_abs2
    br = b_re.astype(f32)
    bi = b_im.astype(f32)
    bbar_r = cr[..., None] * br - ci[..., None] * bi
    bbar_i = cr[..., None] * bi + ci[..., None] * br
    ug = jnp.swapaxes(u, 0, 1).astype(f32).reshape(seq, bsz, SSM_GROUPS, SSM_GROUP)
    bu_r = jnp.einsum('lbgc,gpc->lbgp', ug, bbar_r)
    bu_i = jnp.einsum('lbgc,gpc->lbgp', ug, bbar_i)
    a_shape = (seq, 1, SSM_GROUPS, SSM_STATE)
    _, _, h_r, h_i = lax.associative_scan(
        _complex_linear_combine,
        (jnp.broadcast_to(ar, a_shape), jnp.broadcast_to(ai, a_shape), bu_r, bu_i),
        axis=0)
    y = (jnp.einsum('gcp,lbgp->lbgc', c_re.astype(f32), h_r)
         - jnp.einsum('gcp,lbgp->lbgc', c_im.astype(f32), h_i))
    y = jnp.swapaxes(y.reshape(seq, bsz, SSM_WIDTH), 0, 1).astype(x.dtype) + d_skip * u
    g = jax.nn.gelu(y)
    y = g * jax.nn.sigmoid(g @ w_glu + b_glu)
    return (y * jax.nn.silu(z)) @ w_out

def shared_kv(h, kv_w, pos_k, w1_k, w2_k, pos_v, w1_v, w2_v):
    bsz, seq, _ = h.shape
    kv = (h @ kv_w).reshape(bsz, seq, 2 * N_BRANCH, N_KV_HEADS, HEAD_DIM)
    k_c, v_c, k_s, v_s, k_w, v_w = [kv[:, :, i] for i in range(2 * N_BRANCH)]
    n_cmp = (seq - CMP_BLOCK) // CMP_STRIDE + 1
    idx = jnp.arange(n_cmp)[:, None] * CMP_STRIDE + jnp.arange(CMP_BLOCK)[None, :]

    def compress(t, pos, w1, w2):
        blk = t[:, idx] + pos[None, None, :, None, :]
        blk = jnp.moveaxis(blk, 3, 2).reshape(bsz, n_cmp, N_KV_HEADS, CMP_BLOCK * HEAD_DIM)
        return jax.nn.gelu(blk @ w1) @ w2

    return (compress(k_c, pos_k, w1_k, w2_k), compress(v_c, pos_v, w1_v, w2_v), k_s, v_s, k_w, v_w)

def masked_softmax(s, valid):
    s = jnp.where(valid, s, MASK_VALUE)
    m = jnp.max(s, axis=-1, keepdims=True)
    e = jnp.where(valid, jnp.exp(s - m), 0.0)
    return e / jnp.maximum(jnp.sum(e, axis=-1, keepdims=True), 1e-30)

def nsa_attention(q, k_cmp, v_cmp, k_slc, v_slc, k_win, v_win):
    bsz, seq = q.shape[:2]
    dtype = q.dtype
    f32 = jnp.float32
    n_q = seq // Q_BLOCK
    n_cmp = k_cmp.shape[1]
    n_sblk = seq // SEL_BLOCK
    n_sel = min(N_SELECT, n_sblk)
    scale = HEAD_DIM ** -0.5
    cmp_start = jnp.arange(n_cmp) * CMP_STRIDE
    cmp_end = cmp_start + CMP_BLOCK - 1
    sel_start = jnp.arange(n_sblk) * SEL_BLOCK
    overlap = ((cmp_start[:, None] < sel_start[None, :] + SEL_BLOCK)
               & (cmp_end[:, None] >= sel_start[None, :])).astype(f32)
    kb_s = k_slc.reshape(bsz, n_sblk, SEL_BLOCK, N_KV_HEADS, HEAD_DIM).transpose(0, 3, 1, 2, 4)
    vb_s = v_slc.reshape(bsz, n_sblk, SEL_BLOCK, N_KV_HEADS, HEAD_DIM).transpose(0, 3, 1, 2, 4)
    k_w_pad = jnp.pad(k_win, ((0, 0), (WINDOW, 0), (0, 0), (0, 0)))
    v_w_pad = jnp.pad(v_win, ((0, 0), (WINDOW, 0), (0, 0), (0, 0)))
    qg = q.reshape(bsz, n_q, Q_BLOCK, N_KV_HEADS, HEADS_PER_KV, HEAD_DIM).transpose(1, 0, 2, 3, 4, 5)
    gather_blocks = jax.vmap(jax.vmap(lambda blocks, ids: blocks[ids]))
    blk_ids = jnp.arange(n_sblk)

    def block_fn(args):
        i, qb = args
        t = i * Q_BLOCK + jnp.arange(Q_BLOCK)
        qb = qb * scale
        s = jnp.einsum('bqghd,bngd->bghqn', qb, k_cmp).astype(f32)
        p_cmp = masked_softmax(s, cmp_end[None, :] <= t[:, None])
        o_cmp = jnp.einsum('bghqn,bngd->bqghd', p_cmp.astype(dtype), v_cmp)
        imp = jnp.einsum('bghqn,nj->bgqj', p_cmp, overlap)
        cur = t // SEL_BLOCK
        future = blk_ids[None, :] > cur[:, None]
        forced = ((blk_ids[None, :] == 0) | (blk_ids[None, :] == cur[:, None])
                  | (blk_ids[None, :] == cur[:, None] - 1))
        imp = jnp.where(future, MASK_VALUE, jnp.where(forced, FORCE_SCORE, imp))
        _, sel = lax.top_k(imp, n_sel)
        ks = gather_blocks(kb_s, sel).reshape(bsz, N_KV_HEADS, Q_BLOCK, n_sel * SEL_BLOCK, HEAD_DIM)
        vs = gather_blocks(vb_s, sel).reshape(bsz, N_KV_HEADS, Q_BLOCK, n_sel * SEL_BLOCK, HEAD_DIM)
        pos = (sel[..., None] * SEL_BLOCK + jnp.arange(SEL_BLOCK)).reshape(bsz, N_KV_HEADS, Q_BLOCK, n_sel * SEL_BLOCK)
        valid = (pos <= t[None, None, :, None])[:, :, None]
        s = jnp.einsum('bqghd,bgqkd->bghqk', qb, ks).astype(f32)
        p = masked_softmax(s, valid)
        o_slc = jnp.einsum('bghqk,bgqkd->bqghd', p.astype(dtype), vs)
        kw = lax.dynamic_slice_in_dim(k_w_pad, i * Q_BLOCK, WINDOW + Q_BLOCK, axis=1)
        vw = lax.dynamic_slice_in_dim(v_w_pad, i * Q_BLOCK, WINDOW + Q_BLOCK, axis=1)
        kpos = i * Q_BLOCK - WINDOW + jnp.arange(WINDOW + Q_BLOCK)
        valid = ((kpos[None, :] <= t[:, None]) & (kpos[None, :] > t[:, None] - WINDOW)
                 & (kpos[None, :] >= 0))
        s = jnp.einsum('bqghd,bkgd->bghqk', qb, kw).astype(f32)
        p = masked_softmax(s, valid)
        o_win = jnp.einsum('bghqk,bkgd->bqghd', p.astype(dtype), vw)
        return o_cmp, o_slc, o_win

    o_cmp, o_slc, o_win = lax.map(block_fn, (jnp.arange(n_q), qg))

    def unblock(o):
        return o.transpose(1, 0, 2, 3, 4, 5).reshape(bsz, seq, N_HEADS, HEAD_DIM)

    return (unblock(o_cmp), unblock(o_slc), unblock(o_win))

def nsa_mixer(x, w_in, w_out, shared):
    bsz, seq, _ = x.shape
    proj = x @ w_in
    q = proj[..., :ATTN_WIDTH].reshape(bsz, seq, N_HEADS, HEAD_DIM)
    z = proj[..., ATTN_WIDTH:ATTN_WIDTH * (1 + N_BRANCH)].reshape(bsz, seq, N_BRANCH, N_HEADS, HEAD_DIM)
    gate = jax.nn.sigmoid(proj[..., ATTN_WIDTH * (1 + N_BRANCH):].reshape(bsz, seq, N_BRANCH, N_HEADS))
    o = jnp.stack(nsa_attention(q, *shared), axis=2)
    y = jnp.sum(gate[..., None] * o * jax.nn.silu(z), axis=2).reshape(bsz, seq, ATTN_WIDTH)
    return y @ w_out

def first_inputs(seed: int = 0) -> dict:
    key = jax.random.key(seed)
    ks = jax.random.split(key, 24)
    nrm = jax.random.normal
    f32 = jnp.float32
    na, nb = N_A_LAYERS, N_B_LAYERS
    g, p, c, e = SSM_GROUPS, SSM_STATE, SSM_GROUP, SSM_WIDTH
    lam_im0 = math.pi * jnp.arange(p, dtype=f32)
    return {
        "x": nrm(ks[0], (BATCH, SEQ, D_MODEL), f32),
        "a_w_in": nrm(ks[1], (na, D_MODEL, 2 * e), f32) * D_MODEL ** -0.5,
        "a_lam_re": -0.5 + 0.01 * nrm(ks[2], (na, g, p), f32),
        "a_lam_im": lam_im0 + 0.01 * nrm(ks[3], (na, g, p), f32),
        "a_log_dt": jax.random.uniform(ks[4], (na, g), f32, math.log(DT_MIN), math.log(DT_MAX)),
        "a_b_re": nrm(ks[5], (na, g, p, c), f32) * (2 * c) ** -0.5,
        "a_b_im": nrm(ks[6], (na, g, p, c), f32) * (2 * c) ** -0.5,
        "a_c_re": nrm(ks[7], (na, g, c, p), f32) * p ** -0.5,
        "a_c_im": nrm(ks[8], (na, g, c, p), f32) * p ** -0.5,
        "a_d": nrm(ks[9], (na, e), f32),
        "a_w_glu": nrm(ks[10], (na, e, e), f32) * e ** -0.5,
        "a_b_glu": 0.01 * nrm(ks[11], (na, e), f32),
        "a_w_out": nrm(ks[12], (na, e, D_MODEL), f32) * e ** -0.5 * DEEPNORM_BETA,
        "kv_w": nrm(ks[13], (D_MODEL, 2 * N_BRANCH * KV_WIDTH), f32) * D_MODEL ** -0.5,
        "cmp_pos_k": 0.02 * nrm(ks[14], (CMP_BLOCK, HEAD_DIM), f32),
        "cmp_w1_k": nrm(ks[15], (CMP_BLOCK * HEAD_DIM, HEAD_DIM), f32) * (CMP_BLOCK * HEAD_DIM) ** -0.5,
        "cmp_w2_k": nrm(ks[16], (HEAD_DIM, HEAD_DIM), f32) * HEAD_DIM ** -0.5,
        "cmp_pos_v": 0.02 * nrm(ks[17], (CMP_BLOCK, HEAD_DIM), f32),
        "cmp_w1_v": nrm(ks[18], (CMP_BLOCK * HEAD_DIM, HEAD_DIM), f32) * (CMP_BLOCK * HEAD_DIM) ** -0.5,
        "cmp_w2_v": nrm(ks[19], (HEAD_DIM, HEAD_DIM), f32) * HEAD_DIM ** -0.5,
        "b_w_in": nrm(ks[20], (nb, D_MODEL, B_IN_WIDTH), f32) * D_MODEL ** -0.5,
        "b_w_out": nrm(ks[21], (nb, ATTN_WIDTH, D_MODEL), f32) * ATTN_WIDTH ** -0.5 * DEEPNORM_BETA,
        "ln_g": 1.0 + 0.01 * nrm(ks[22], (DEPTH, D_MODEL), f32),
        "ln_b": 0.01 * nrm(ks[23], (DEPTH, D_MODEL), f32),
    }

def first_block(x, a_w_in, a_lam_re, a_lam_im, a_log_dt, a_b_re, a_b_im, a_c_re, a_c_im, a_d,
              a_w_glu, a_b_glu, a_w_out, kv_w, cmp_pos_k, cmp_w1_k, cmp_w2_k, cmp_pos_v,
              cmp_w1_v, cmp_w2_v, b_w_in, b_w_out, ln_g, ln_b):
    shared = None
    for layer in range(DEPTH):
        if layer < N_A_LAYERS:
            i = layer
            y = s5_mixer(x, a_w_in[i], a_lam_re[i], a_lam_im[i], a_log_dt[i], a_b_re[i], a_b_im[i],
                         a_c_re[i], a_c_im[i], a_d[i], a_w_glu[i], a_b_glu[i], a_w_out[i])
        else:
            i = layer - N_A_LAYERS
            y = nsa_mixer(x, b_w_in[i], b_w_out[i], shared)
        x = layer_norm(DEEPNORM_ALPHA * x + y, ln_g[layer], ln_b[layer])
        if layer == N_A_LAYERS - 1:
            shared = shared_kv(x, kv_w, cmp_pos_k, cmp_w1_k, cmp_w2_k, cmp_pos_v, cmp_w1_v, cmp_w2_v)
    return x


DEPTH_2 = 1

EPS = 1e-6
CHUNK = 64

A_HEADS = 8
A_DK = 128
A_DV = 128
A_WIDTH = A_HEADS * A_DV

B_QK_HEADS = 4
B_V_HEADS = 8
B_DK = 128
B_DV = 128
B_WIDTH = B_V_HEADS * B_DV
CONV = 4
B_CONV_CH = 2 * B_QK_HEADS * B_DK + B_WIDTH

MIX_WIDTH = A_WIDTH + B_WIDTH

IN_SIZES = (A_HEADS * A_DK, A_HEADS * A_DK, A_WIDTH, A_WIDTH,
            B_QK_HEADS * B_DK, B_QK_HEADS * B_DK, B_WIDTH, B_WIDTH,
            B_V_HEADS, B_V_HEADS)
IN_WIDTH = 4 * A_HEADS * A_DK + 2 * B_QK_HEADS * B_DK + 2 * B_WIDTH + 2 * B_V_HEADS

P_HEADS = 8
N_KEYS = 128
N_EXPERTS = N_KEYS * N_KEYS
P_DKEY = 256
P_TOPK = 16
P_BLOCK = 128


def _rmsnorm(x, g):
    xf = x.astype(jnp.float32)
    y = xf * lax.rsqrt(jnp.mean(xf * xf, axis=-1, keepdims=True) + EPS)
    return (y * g.astype(jnp.float32)).astype(x.dtype)

def _gated_rmsnorm(o, z, g):
    of = o.astype(jnp.float32)
    y = of * lax.rsqrt(jnp.mean(of * of, axis=-1, keepdims=True) + EPS)
    return y * g.astype(jnp.float32) * jax.nn.silu(z.astype(jnp.float32))

def _l2norm(x):
    xf = x.astype(jnp.float32)
    return xf * lax.rsqrt(jnp.sum(xf * xf, axis=-1, keepdims=True) + EPS)

def _chunk(t):
    b, s, h = t.shape[:3]
    rest = t.shape[3:]
    t = t.reshape((b, s // CHUNK, CHUNK, h) + rest)
    return t.transpose((1, 0, 3, 2) + tuple(range(4, t.ndim)))

def _unchunk(t):
    n, b, h, c, d = t.shape
    return t.transpose(1, 0, 3, 2, 4).reshape(b, n * c, h, d)

def _causal_conv_silu(x, w):
    s = x.shape[1]
    xp = jnp.pad(x, ((0, 0), (CONV - 1, 0), (0, 0)))
    y = xp[:, 0:s, :] * w[0]
    for j in range(1, CONV):
        y = y + xp[:, j:j + s, :] * w[j]
    return jax.nn.silu(y)

def _hgrn2(q, f_logit, v, lb):
    q = q.astype(jnp.float32)
    z = f_logit.astype(jnp.float32)
    v = v.astype(jnp.float32)
    lb = lb.astype(jnp.float32)
    log_f = jnp.log(lb + (1.0 - lb) * jax.nn.sigmoid(z))
    k = (1.0 - lb) * jax.nn.sigmoid(-z)
    qc, kc, vc = _chunk(q), _chunk(k), _chunk(v)
    bc = jnp.cumsum(_chunk(log_f), axis=-2)
    causal = jnp.tril(jnp.ones((CHUNK, CHUNK), dtype=bool))

    def step(S, inp):
        q_c, k_c, v_c, b_c = inp
        diff = b_c[..., :, None, :] - b_c[..., None, :, :]
        decay = jnp.exp(jnp.where(causal[:, :, None], diff, -jnp.inf))
        att = jnp.einsum('bhtd,bhsd,bhtsd->bhts', q_c, k_c, decay)
        o = (jnp.einsum('bhtd,bhdv->bhtv', q_c * jnp.exp(b_c), S)
             + jnp.einsum('bhts,bhsv->bhtv', att, v_c))
        b_last = b_c[..., -1:, :]
        S = (S * jnp.exp(b_last[..., 0, :, None])
             + jnp.einsum('bhsd,bhsv->bhdv', k_c * jnp.exp(b_last - b_c), v_c))
        return S, o

    S0 = jnp.zeros((q.shape[0], q.shape[2], A_DK, A_DV), jnp.float32)
    _, o = lax.scan(step, S0, (qc, kc, vc, bc))
    return _unchunk(o)

def _gated_delta(q, k, v, beta, g):
    q = _chunk(q.astype(jnp.float32) * (B_DK ** -0.5))
    k = _chunk(k.astype(jnp.float32))
    v = _chunk(v.astype(jnp.float32))
    beta = _chunk(beta.astype(jnp.float32))
    gc = jnp.cumsum(_chunk(g.astype(jnp.float32)), axis=-1)
    incl = jnp.tril(jnp.ones((CHUNK, CHUNK), dtype=bool))
    strict = jnp.tril(jnp.ones((CHUNK, CHUNK), dtype=bool), k=-1)
    L = jnp.exp(jnp.where(incl, gc[..., :, None] - gc[..., None, :], -jnp.inf))
    kb = k * beta[..., None]
    M = jnp.eye(CHUNK, dtype=jnp.float32) + jnp.where(
        strict, jnp.einsum('...td,...sd->...ts', kb, k) * L, 0.0)
    u = lax.linalg.triangular_solve(M, v * beta[..., None], left_side=True,
                                    lower=True, unit_diagonal=True)
    w = lax.linalg.triangular_solve(M, kb * jnp.exp(gc)[..., None], left_side=True,
                                    lower=True, unit_diagonal=True)
    a_qk = jnp.einsum('...td,...sd->...ts', q, k) * L
    qg = q * jnp.exp(gc)[..., None]
    g_last = gc[..., -1:]
    kd = k * jnp.exp(g_last - gc)[..., None]
    dl = jnp.exp(g_last)[..., None]

    def step(S, inp):
        qg_c, kd_c, u_c, w_c, a_c, dl_c = inp
        v_new = u_c - jnp.einsum('bhtd,bhdv->bhtv', w_c, S)
        o = (jnp.einsum('bhtd,bhdv->bhtv', qg_c, S)
             + jnp.einsum('bhts,bhsv->bhtv', a_c, v_new))
        S = S * dl_c + jnp.einsum('bhsd,bhsv->bhdv', kd_c, v_new)
        return S, o

    S0 = jnp.zeros((qg.shape[1], qg.shape[2], B_DK, B_DV), jnp.float32)
    _, o = lax.scan(step, S0, (qg, kd, u, w, a_qk, dl))
    return _unchunk(o)

def _peer(xn, w_query, sub_keys, u_tab, v_tab):
    b, s, d = xn.shape
    t = b * s
    xt = xn.reshape(t, d)
    qry = jnp.einsum('td,dhk->thk', xt, w_query).astype(jnp.float32)
    half = P_DKEY // 2
    s1 = jnp.einsum('thk,hnk->thn', qry[..., :half], sub_keys[0].astype(jnp.float32))
    s2 = jnp.einsum('thk,hnk->thn', qry[..., half:], sub_keys[1].astype(jnp.float32))
    v1, i1 = lax.top_k(s1, P_TOPK)
    v2, i2 = lax.top_k(s2, P_TOPK)
    cand = (v1[..., :, None] + v2[..., None, :]).reshape(t, P_HEADS, P_TOPK * P_TOPK)
    best, pos = lax.top_k(cand, P_TOPK)
    expert = (jnp.take_along_axis(i1, pos // P_TOPK, axis=-1) * N_KEYS
              + jnp.take_along_axis(i2, pos % P_TOPK, axis=-1))
    gate = jax.nn.softmax(best, axis=-1)
    nblk = t // P_BLOCK

    def blk(args):
        xb, eb, gb = args
        hid = jax.nn.gelu(jnp.einsum('pd,phkd->phk', xb, u_tab[eb]).astype(jnp.float32),
                          approximate=False)
        return jnp.einsum('phk,phkd->pd', (gb * hid).astype(xb.dtype), v_tab[eb])

    y = lax.map(blk, (xt.reshape(nblk, P_BLOCK, d),
                      expert.reshape(nblk, P_BLOCK, P_HEADS, P_TOPK),
                      gate.reshape(nblk, P_BLOCK, P_HEADS, P_TOPK)))
    return y.reshape(b, s, d)

def second_inputs(seed: int = 0) -> dict:
    key = jax.random.key(seed)
    ks = jax.random.split(key, 20)
    f32 = jnp.float32
    nrm = lambda k, shape, scale: jax.random.normal(k, shape, f32) * scale
    gain = lambda k, shape: 1.0 + 0.02 * jax.random.normal(k, shape, f32)
    dt = jnp.exp(jax.random.uniform(ks[8], (DEPTH_2, B_V_HEADS), f32,
                                    minval=np.log(1e-3), maxval=np.log(1e-1)))
    return {
        "x": nrm(ks[0], (BATCH, SEQ, D_MODEL), 1.0),
        "attn_norm_g": gain(ks[1], (DEPTH_2, D_MODEL)),
        "w_in": nrm(ks[2], (DEPTH_2, D_MODEL, IN_WIDTH), D_MODEL ** -0.5),
        "hgrn_lb_logits": nrm(ks[3], (DEPTH_2 + 1, A_HEADS, A_DK), 0.1),
        "hgrn_norm_g": gain(ks[4], (DEPTH_2, A_DV)),
        "gdn_conv_w": nrm(ks[5], (DEPTH_2, CONV, B_CONV_CH), CONV ** -0.5),
        "gdn_A_log": jnp.log(jax.random.uniform(ks[6], (DEPTH_2, B_V_HEADS), f32,
                                                minval=1.0, maxval=16.0)),
        "gdn_dt_bias": dt + jnp.log(-jnp.expm1(-dt)),
        "gdn_norm_g": gain(ks[7], (DEPTH_2, B_DV)),
        "w_out": nrm(ks[9], (DEPTH_2, MIX_WIDTH, D_MODEL), MIX_WIDTH ** -0.5),
        "ffn_norm_g": gain(ks[10], (DEPTH_2, D_MODEL)),
        "peer_w_query": nrm(ks[11], (DEPTH_2, D_MODEL, P_HEADS, P_DKEY), D_MODEL ** -0.5),
        "peer_sub_keys": nrm(ks[12], (DEPTH_2, 2, P_HEADS, N_KEYS, P_DKEY // 2),
                             (P_DKEY // 2) ** -0.5),
        "peer_u": nrm(ks[13], (DEPTH_2, N_EXPERTS, D_MODEL), D_MODEL ** -0.5),
        "peer_v": nrm(ks[14], (DEPTH_2, N_EXPERTS, D_MODEL), P_HEADS ** -0.5),
        "final_norm_g": gain(ks[15], (D_MODEL,)),
    }

def second_block(x, attn_norm_g, w_in, hgrn_lb_logits, hgrn_norm_g, gdn_conv_w, gdn_A_log,
              gdn_dt_bias, gdn_norm_g, w_out, ffn_norm_g, peer_w_query, peer_sub_keys,
              peer_u, peer_v, final_norm_g):
    b, s, _ = x.shape
    lb_all = jnp.cumsum(jax.nn.softmax(hgrn_lb_logits.astype(jnp.float32), axis=0), axis=0)
    offs = []
    acc = 0
    for n in IN_SIZES[:-1]:
        acc += n
        offs.append(acc)
    rep = B_V_HEADS // B_QK_HEADS
    h = x
    for l in range(DEPTH_2):
        xn = _rmsnorm(h, attn_norm_g[l])
        proj = xn @ w_in[l]
        a_q, a_f, a_i, a_g, b_q, b_k, b_v, b_z, b_b, b_a = jnp.split(proj, offs, axis=-1)
        o_a = _hgrn2(a_q.reshape(b, s, A_HEADS, A_DK), a_f.reshape(b, s, A_HEADS, A_DK),
                     a_i.reshape(b, s, A_HEADS, A_DV), lb_all[l])
        o_a = _gated_rmsnorm(o_a, a_g.reshape(b, s, A_HEADS, A_DV), hgrn_norm_g[l])
        qkv = _causal_conv_silu(jnp.concatenate([b_q, b_k, b_v], axis=-1), gdn_conv_w[l])
        nqk = B_QK_HEADS * B_DK
        gq = _l2norm(qkv[..., :nqk].reshape(b, s, B_QK_HEADS, B_DK))
        gk = _l2norm(qkv[..., nqk:2 * nqk].reshape(b, s, B_QK_HEADS, B_DK))
        gv = qkv[..., 2 * nqk:].reshape(b, s, B_V_HEADS, B_DV)
        gq = jnp.repeat(gq, rep, axis=2)
        gk = jnp.repeat(gk, rep, axis=2)
        beta = jax.nn.sigmoid(b_b.astype(jnp.float32))
        g = -jnp.exp(gdn_A_log[l].astype(jnp.float32)) * jax.nn.softplus(
            b_a.astype(jnp.float32) + gdn_dt_bias[l].astype(jnp.float32))
        o_b = _gated_delta(gq, gk, gv, beta, g)
        o_b = _gated_rmsnorm(o_b, b_z.reshape(b, s, B_V_HEADS, B_DV), gdn_norm_g[l])
        mix = jnp.concatenate([o_a.reshape(b, s, A_WIDTH), o_b.reshape(b, s, B_WIDTH)],
                              axis=-1).astype(x.dtype)
        h = h + mix @ w_out[l]
        hn = _rmsnorm(h, ffn_norm_g[l])
        h = h + _peer(hn, peer_w_query[l], peer_sub_keys[l], peer_u[l], peer_v[l])
    return _rmsnorm(h, final_norm_g)


def setup_inputs(seed=0):
    out = dict(first_inputs(seed))
    for name, value in second_inputs(seed + 1).items():
        if name != "x":
            out[name + "_2"] = value
    return out


def reference(
    x, a_w_in, a_lam_re, a_lam_im, a_log_dt, a_b_re, a_b_im, a_c_re, a_c_im, a_d, a_w_glu,
    a_b_glu, a_w_out, kv_w, cmp_pos_k, cmp_w1_k, cmp_w2_k, cmp_pos_v, cmp_w1_v, cmp_w2_v,
    b_w_in, b_w_out, ln_g, ln_b, attn_norm_g_2, w_in_2, hgrn_lb_logits_2, hgrn_norm_g_2,
    gdn_conv_w_2, gdn_A_log_2, gdn_dt_bias_2, gdn_norm_g_2, w_out_2, ffn_norm_g_2,
    peer_w_query_2, peer_sub_keys_2, peer_u_2, peer_v_2, final_norm_g_2,
):
    x = first_block(
        x, a_w_in, a_lam_re, a_lam_im, a_log_dt, a_b_re, a_b_im, a_c_re, a_c_im, a_d, a_w_glu,
        a_b_glu, a_w_out, kv_w, cmp_pos_k, cmp_w1_k, cmp_w2_k, cmp_pos_v, cmp_w1_v, cmp_w2_v,
        b_w_in, b_w_out, ln_g, ln_b,
    )
    return second_block(
        x, attn_norm_g_2, w_in_2, hgrn_lb_logits_2, hgrn_norm_g_2, gdn_conv_w_2, gdn_A_log_2,
        gdn_dt_bias_2, gdn_norm_g_2, w_out_2, ffn_norm_g_2, peer_w_query_2, peer_sub_keys_2,
        peer_u_2, peer_v_2, final_norm_g_2,
    )


_drawn_inputs = setup_inputs


def setup_inputs(seed=0):
    import zlib

    import numpy as np

    out = dict(_drawn_inputs(seed))
    spreads = {}
    factors = {'a_lam_re': 64.0,
     'a_lam_im': 29.016,
     'a_log_dt': 31.488,
     'a_b_re': 34.808,
     'a_b_im': 36.864,
     'a_c_re': 34.184,
     'a_c_im': 34.304,
     'a_b_glu': 61.037,
     'cmp_pos_k': 64.0,
     'cmp_pos_v': 8.0,
     'hgrn_norm_g_2': 57.886,
     'gdn_norm_g_2': 58.392,
     'final_norm_g_2': 24.596,
     'ffn_norm_g_2': 19.873}
    for name, (base, spread) in spreads.items():
        noise = np.random.default_rng([zlib.crc32(name.encode()), seed]).standard_normal(out[name].shape)
        drawn = base * np.exp(spread * noise) if base else spread * noise
        out[name] = jnp.asarray(drawn.astype(out[name].dtype))
    for name, factor in factors.items():
        out[name] = (out[name] * factor).astype(out[name].dtype)
    return out
```

```python
from contextlib import ExitStack

import numpy as np
import concourse.bass as bass
from concourse import mybir

F32 = mybir.dt.float32
F32R = mybir.dt.float32r
BF16 = mybir.dt.bfloat16
U32 = mybir.dt.uint32
ALU = mybir.AluOpType
ACT = mybir.ActivationFunctionType
AX = mybir.AxisListType

P = 128
T = 256
TT = T // P
D = 2048
KC = D // P
PIECES = 4
PIECE = 1024
RAW = 3
SLOTS = 6
BANKS = 3
BANK = 512

E = D // 2
GROUPS, STATE, GCH = 64, 64, 16
STILES = GROUPS * STATE // P
ECH = E // P

HEADS, KVH, HD = 16, 4, 128
NCMP, CSTRIDE, CBLOCK = (T - 32) // 16 + 1, 16, 32
SCALE = float(HD) ** -0.5
NEG = -1e30
LN_EPS = 1e-5
ALPHA = 4.0 ** 0.25

EPS = 1e-6
AH = 8
CH = 32
NCH = P // CH
BVH, BQH = 8, 4
PH, NKEY, TOPK = 8, 128, 16

N_A_IN, N_GLU, N_A_OUT, N_KV, N_B_IN, N_B_OUT, N_IN2, N_OUT2, N_WQ = 8, 2, 4, 12, 32, 8, 28, 8, 8
AT_A_IN = 0
AT_GLU = AT_A_IN + N_A_IN
AT_A_OUT = AT_GLU + N_GLU
AT_KV = AT_A_OUT + N_A_OUT
AT_B_IN = AT_KV + N_KV
AT_B_OUT = AT_B_IN + N_B_IN
AT_IN2 = AT_B_OUT + N_B_OUT
AT_OUT2 = AT_IN2 + N_IN2
AT_WQ = AT_OUT2 + N_OUT2
AT_EXPERTS = AT_WQ + N_WQ
PAIRS = 64
N_TILES = AT_EXPERTS + 2 * PAIRS

MEM = 45776
CONSTS = 656
RING0 = CONSTS
LOW0 = RING0 + RAW * PIECE
WORK0 = LOW0 + SLOTS * PIECE // 2
X_HIGH = SLOTS * PIECE
SMALL_HIGH = X_HIGH + KC * T
ROUNDED = SMALL_HIGH + 1024


def tops(w, a, b):
    return w.bitcast(BF16)[:, 2 * a + 1:2 * b:2]


def channel_products(w, x, ws, xs):
    (wh, wl), (xh, xl) = w, x
    return ((wh[:, ws], xh[:, xs]), (wl[:, ws], tops(xh, xs.start, xs.stop)),
            (tops(wh, ws.start, ws.stop), xl[:, xs]))


def token_products(w, x, ws, xs):
    return tuple((b, a) for a, b in channel_products(w, x, ws, xs))


class Steps:

    def __init__(self, eng, own):
        self.eng, self.own, self.n = eng, own, {}

    def __call__(self, ins, sem=None):
        sem = self.own if sem is None else sem
        key = id(sem)
        self.n[key] = self.n.get(key, 0) + 1
        ins.then_inc(sem, 1)
        self.eng.wait_ge(sem, self.n[key])


class Kernel:
    def __init__(self, nc, ctx, ins, out):
        self.nc, self.ctx, self.ins, self.out, self.part = nc, ctx, ins, out, []
        self.mem = ctx.enter_context(nc.sbuf_tensor("mem", [P, MEM], F32))
        self.rounded = ctx.enter_context(nc.sbuf_tensor("rounded", [P, ROUNDED], F32R))
        self.ps = ctx.enter_context(nc.psum_tensor("ps", [P, 8, BANK], F32))
        self.landed = [self.sem(f"piece_landed_{s}") for s in range(RAW)]
        self.high_done = self.sem("high_done")
        self.low_done = self.sem("low_done")
        self.multiplied = self.sem("multiplied")
        self.bank_free = self.sem("bank_free")
        self.issued = 0
        self.vstep, self.astep, self.gstep = self.sem("vector_step"), self.sem("scalar_step"), self.sem("pool_step")
        self.steps = {}
        self.ident = self.at(-WORK0, P)
        self.iota = self.at(P - WORK0, P)
        self.spare = self.at(2 * P - WORK0, 8)
        self.phase = 0
        self.part = []

    def sem(self, name):
        handle = self.nc.alloc_semaphore(name)
        self.part.append(handle)
        return handle

    def new_part(self):
        self.nc.clear_and_free_semaphores(self.part)
        self.nc.all_engine_barrier()
        self.part = []
        for s in self.steps.values():
            s.n = {id(s.own): s.n.get(id(s.own), 0)}

    def at(self, off, n):
        assert WORK0 + off + n <= MEM, (off, n)
        return self.mem[:, WORK0 + off:WORK0 + off + n]

    def split_x(self, low, at=0, n=KC * T):
        return self.rounded[:, X_HIGH + at:X_HIGH + at + n], self.at(low, n // 2).bitcast(BF16)

    def split_small(self, low, n, at=0):
        return self.rounded[:, SMALL_HIGH + at:SMALL_HIGH + at + n], self.at(low, n // 2).bitcast(BF16)

    def raw(self, s):
        return self.mem[:, RING0 + s * PIECE:RING0 + (s + 1) * PIECE]

    def parts(self, s):
        low = LOW0 + s * PIECE // 2
        return self.rounded[:, s * PIECE:(s + 1) * PIECE], self.mem[:, low:low + PIECE // 2].bitcast(BF16)

    def stepper(self, eng, own):
        key = id(own)
        if key not in self.steps:
            self.steps[key] = Steps(eng, own)
        self.steps[key].eng = eng
        return self.steps[key]

    def stream(self, sp, upto, ahead=True):
        upto = min(PIECES * upto + (RAW if ahead else 0), PIECES * N_TILES)
        while self.issued < upto:
            i = self.issued
            name, first, end = (("weights", 0, PIECES * AT_EXPERTS) if i < PIECES * AT_EXPERTS else
                                ("experts", PIECES * AT_EXPERTS, PIECES * N_TILES))
            src = self.ins[name]
            end = min(end, upto)
            groups = (end - i) // RAW
            if i >= RAW and groups >= 2:
                with sp.Fori(0, groups) as g:
                    for j in range(RAW):
                        sp.wait_ge(self.low_done, g * RAW + (i + j - RAW + 1))
                        sp.dma_start(self.raw((i + j) % RAW),
                                     src[bass.ds(g * RAW + (i + j - first), 1)].rearrange("a p n -> (a p) n")
                                     ).then_inc(self.landed[(i + j) % RAW], 16)
                self.issued += groups * RAW
            else:
                if i >= RAW:
                    sp.wait_ge(self.low_done, i - RAW + 1)
                sp.dma_start(self.raw(i % RAW), src[i - first]).then_inc(self.landed[i % RAW], 16)
                self.issued += 1

    def high(self, act, c, m=0, per=0):
        act.wait_ge(self.landed[c % RAW], (m * (per // RAW) + (c // RAW + 1)) * 16)
        if c >= SLOTS:
            act.wait_ge(self.multiplied, m * per + (c - SLOTS + 1))
        self.nc.scalar.copy(self.parts(c % SLOTS)[0], self.raw(c % RAW)).then_inc(self.high_done, 1)

    def low(self, dve, c, m=0, per=0):
        wh, wl = self.parts(c % SLOTS)
        dve.wait_ge(self.high_done, m * per + (c + 1))
        self.nc.vector.tensor_tensor(wl, self.raw(c % RAW), wh.bitcast(F32), ALU.subtract).then_inc(self.low_done, 1)

    def tiles(self, eng, n, body, loop=True):
        groups = n // BANKS if loop else 0
        done = 0
        if groups >= 2:
            with eng.Fori(0, groups) as g:
                for j in range(BANKS):
                    body(g * BANKS + j, j, g)
            done = groups * BANKS
        for j in range(done, n):
            body(j, j, 0)

    def multiply(self, pe, first, n, act, kind):
        nc, ps = self.nc, self.ps
        products = channel_products if kind == "channel" else token_products

        def body(t, j, g):
            bank = (first + j) % BANKS
            pe.wait_ge(self.bank_free, g * BANKS + (first + j + 1))
            for part in range(PIECES):
                c = PIECES * (first + j) + part
                pe.wait_ge(self.low_done, g * PIECES * BANKS + (c + 1))
                for half in range(2):
                    for kk in range(KC // PIECES):
                        kc = part * (KC // PIECES) + kk
                        if kind == "channel":
                            ws = slice(kk * 256 + half * P, kk * 256 + half * P + P)
                            xs = slice(kc * T, (kc + 1) * T)
                        else:
                            ws = slice(kk * 256, (kk + 1) * 256)
                            xs = slice(kc * T + half * P, kc * T + half * P + P)
                        for i, (a, b) in enumerate(products(self.parts(c % SLOTS), act, ws, xs)):
                            mm = nc.tensor.matmul(ps[:, bank, half * 256:half * 256 + 256], a, b,
                                                  start=(kc == 0 and half == 0 and i == 0),
                                                  stop=(kc == KC - 1 and half == 1 and i == 2), skip_group_check=True)
                mm.then_inc(self.multiplied, 1)

        self.tiles(pe, n, body)

    def split_and_drain(self, eng, first, n, split, emit=None):
        def pieces(c, g):
            for part in range(PIECES):
                split(eng, PIECES * (first + c) + part, g, PIECES * BANKS)

        def drain(t, j, g):
            if emit:
                eng.wait_ge(self.multiplied, g * PIECES * BANKS + PIECES * (first + j + 1))
                emit((first + j) % BANKS, t).then_inc(self.bank_free, 1)

        def body(t, j, g):
            pieces(j + 1, g)
            drain(t, j, g)

        pieces(0, 0)
        self.tiles(eng, n - 1, body, first > 0)
        drain(n - 1, n - 1, 0)

    def transposes(self, src, dst, upto, head=None):
        nc, ps = self.nc, self.ps
        self.phase += 1
        full, copied = self.sem(f"turned_{self.phase}"), self.sem(f"turned_out_{self.phase}")
        with nc.Block() as block:
            @block.sync
            def _(sp):
                self.stream(sp, upto)

            ready = head(block) if head else []

            @block.tensor
            def _(pe):
                for sem, value in ready:
                    pe.wait_ge(sem, value)
                for b in range(8):
                    for c in range(2):
                        for tt in range(TT):
                            kc = 2 * b + c
                            mm = nc.tensor.transpose(ps[:, b, c * T + tt * P:c * T + tt * P + P],
                                                     src[:, tt * D + kc * P:tt * D + kc * P + P], self.ident)
                    mm.then_inc(full, 1)

            dh, dl = dst

            @block.scalar
            def _(act):
                for b in range(8):
                    act.wait_ge(full, b + 1)
                    nc.scalar.copy(dh[:, b * BANK:(b + 1) * BANK], ps[:, b, :]).then_inc(copied, 1)

            @block.vector
            def _(dve):
                for b in range(8):
                    dve.wait_ge(copied, b + 1)
                    nc.vector.tensor_tensor(dl[:, b * BANK:(b + 1) * BANK], ps[:, b, :],
                                            dh[:, b * BANK:(b + 1) * BANK].bitcast(F32), ALU.subtract)

    def layer_norm(self, x, out, layer, g, b, st, dst, upto):
        nc = self.nc

        def head(block):
            rows, var, root, normed = (self.sem(f"{n}_{self.phase}") for n in
                                       ("ln_rows", "ln_var", "ln_root", "ln_done"))

            @block.scalar
            def _(act):
                act.dma_start(g, self.ins["ln_g"][layer]).then_inc(rows, 16)
                act.dma_start(b, self.ins["ln_b"][layer]).then_inc(rows, 16)
                act.wait_ge(var, 1)
                nc.scalar.activation(st[:, 56:58], st[:, 52:54], ACT.Sqrt).then_inc(root, 1)

            @block.vector
            def _(dve):
                v = self.stepper(dve, self.vstep)
                for tt in range(TT):
                    for c in range(4):
                        v(nc.vector.bn_stats(st[:, 24 * tt + 6 * c:24 * tt + 6 * c + 6],
                                             x[:, tt * D + c * 512:tt * D + c * 512 + 512]))
                    v(nc.vector.bn_aggr(st[:, 48 + 2 * tt:50 + 2 * tt], st[:, 24 * tt:24 * tt + 24]))
                nc.vector.tensor_scalar(st[:, 52:54], st[:, 49:52:2], LN_EPS, None, ALU.add).then_inc(var, 1)
                dve.wait_ge(root, 1)
                v(nc.vector.reciprocal(st[:, 58:60], st[:, 56:58]))
                dve.wait_ge(rows, 32)
                for tt in range(TT):
                    xs = x[:, tt * D:(tt + 1) * D]
                    v(nc.vector.tensor_scalar(xs, xs, st[:, 48 + 2 * tt:49 + 2 * tt], st[:, 58 + tt:59 + tt],
                                              ALU.subtract, ALU.mult))
                    v(nc.vector.tensor_tensor(xs, xs, g, ALU.mult))
                    v(nc.vector.tensor_tensor(out[:, tt * D:(tt + 1) * D], xs, b, ALU.add), normed)
            return [(normed, TT)]

        if dst is not None:
            self.transposes(out, dst, upto, head)
            return
        self.phase += 1
        with nc.Block() as block:
            head(block)

    def rms_scale(self, block, h, gname, g, st, out, tag, signal):
        nc = self.nc
        rows, sums, msq, root = (self.sem(f"{n}_{tag}") for n in ("rms_row", "rms_sums", "rms_mean", "rms_root"))

        @block.scalar
        def _(act):
            a = self.stepper(act, self.astep)
            act.dma_start(g, self.ins[gname]).then_inc(rows, 16)
            for tt in range(TT):
                a(nc.scalar.activation(out[:, tt * D:(tt + 1) * D], h[:, tt * D:(tt + 1) * D], ACT.Square,
                                       accum_out=st[:, tt:tt + 1]), sums)
            act.wait_ge(msq, 1)
            nc.scalar.activation(st[:, 4:6], st[:, 2:4], ACT.Sqrt).then_inc(root, 1)

        @block.vector
        def _(dve):
            v = self.stepper(dve, self.vstep)
            dve.wait_ge(sums, TT)
            nc.vector.tensor_scalar(st[:, 2:4], st[:, 0:2], 1.0 / D, EPS, ALU.mult, ALU.add).then_inc(msq, 1)
            dve.wait_ge(root, 1)
            v(nc.vector.reciprocal(st[:, 6:8], st[:, 4:6]))
            dve.wait_ge(rows, 16)
            for tt in range(TT):
                v(nc.vector.scalar_tensor_tensor(out=out[:, tt * D:(tt + 1) * D], in0=h[:, tt * D:(tt + 1) * D],
                                                 scalar=st[:, 6 + tt:7 + tt], in1=g, op0=ALU.mult, op1=ALU.mult),
                  signal)

    def project_residual(self, first, n, act, x, scale, dst, upto):
        nc, ps = self.nc, self.ps

        def rows(a, j):
            return a.rearrange("p (a n) -> p a n", a=TT)[:, :, bass.ds(j * 256, 256)]

        with nc.Block() as block:
            @block.sync
            def _(sp):
                self.stream(sp, upto)

            @block.tensor
            def _(pe):
                self.multiply(pe, first, n, act, "token")

            @block.scalar
            def _(act):
                self.split_and_drain(act, first, n, self.high)

            @block.vector
            def _(dve):
                self.split_and_drain(dve, first, n, self.low, lambda s, j: nc.vector.scalar_tensor_tensor(
                    out=rows(dst, j), in0=rows(x, j), scalar=scale,
                    in1=ps[:, s, :].rearrange("p (a n) -> p a n", a=TT), op0=ALU.mult, op1=ALU.add))


MAGIC = float(3 << 22)
TWO_PI = (6.28125, 0.00193500518798828125, 3.0199159819e-07)


def s5_inputs_and_tables(k):
    nc, ps, ins = k.nc, k.ps, k.ins
    uz = k.at(4096, 4096)
    x_raw = k.at(8192, 4096)
    xh, xl = xT = k.split_x(35904)
    x_high, x_low = k.sem("x_high"), k.sem("x_low")
    tc, ts = k.at(8192, 8192), k.at(16384, 8192)
    tc3, ts3 = (a.rearrange("p (i t) -> p i t", t=T) for a in (tc, ts))
    par = k.at(24576, 24 * 32)
    names = ("lr li ldt dt lrdt x r half mag s sh c am1 inv cr ci t0 t1 cm sm cm2 sm2 n t2").split()
    q = {name: par[:, 32 * i:32 * i + 32] for i, name in enumerate(names)}
    bre, bim, cre, cim, bbr, bbi, bt_r, bt_i, ncre, ncim = (k.at(25600 + 1024 * i, 1024) for i in range(10))
    small = k.at(35840, 64)
    tmp_v, tmp_p = k.at(0, 2048), k.at(2048, 2048)
    k.s5 = dict(q=q, cre=cre, ncre=ncre, ncim=ncim, bt_r=bt_r, bt_i=bt_i, small=small)
    loaded, x_in, consts = k.sem("s5_params"), k.sem("x_landed"), k.sem("consts_landed")
    dt_ready, angle, trig, bbar = k.sem("dt_ready"), k.sem("angle_ready"), k.sem("trig_ready"), k.sem("bbar_ready")
    turned, step_z, cos_done, sin_done = k.sem("bbar_turned"), k.sem("phase_steps"), k.sem("cos_level"), k.sem("sin_level")

    with nc.Block() as block:
        @block.sync
        def _(sp):
            sp.dma_start(x_raw, ins["x_t"]).then_inc(x_in, 16)
            k.stream(sp, AT_GLU)

        @block.scalar
        def _(act):
            a = k.stepper(act, k.astep)
            act.dma_start(par[:, 0:96], ins["s5_states"]).then_inc(loaded, 16)
            act.dma_start(k.at(-WORK0, 256), ins["consts"]).then_inc(consts, 16)
            for dst, name in ((bre, "s5_b_re"), (bim, "s5_b_im"), (cre, "s5_c_re"), (cim, "s5_c_im")):
                act.dma_start(dst, ins[name]).then_inc(loaded, 16)
            act.dma_start(small[:, 0:16], ins["s5_channels"]).then_inc(loaded, 16)
            act.wait_ge(x_in, 16)
            a(nc.scalar.copy(xh, x_raw), x_high)
            act.wait_ge(loaded, 96)
            nc.scalar.activation(q["dt"], q["ldt"], ACT.Exp).then_inc(dt_ready, 1)
            act.wait_ge(angle, 1)
            a(nc.scalar.activation(q["mag"], q["lrdt"], ACT.Exp))
            a(nc.scalar.activation(q["s"], q["r"], ACT.Sin))
            a(nc.scalar.activation(q["sh"], q["half"], ACT.Sin), trig)
            a(nc.scalar.mul(ncre, cre, -1.0))
            a(nc.scalar.mul(ncim, cim, -1.0))
            k.split_and_drain(act, AT_A_IN, N_A_IN, k.high,
                              lambda s, j: nc.scalar.copy(uz[:, bass.ds(j * BANK, BANK)], ps[:, s, :]))
            for b, dst in ((4, bt_r[:, 0:512]), (5, bt_r[:, 512:]), (6, bt_i[:, 0:512]), (7, bt_i[:, 512:])):
                act.wait_ge(turned, b - 3)
                a(nc.scalar.copy(dst, ps[:, b, :]))

        @block.tensor
        def _(pe):
            pe.wait_ge(x_low, 1)
            k.multiply(pe, AT_A_IN, N_A_IN, xT, "channel")
            pe.wait_ge(consts, 16)
            pe.wait_ge(bbar, 2)
            for b, src in ((4, bbr[:, 0:512]), (5, bbr[:, 512:]), (6, bbi[:, 0:512]), (7, bbi[:, 512:])):
                for j in range(4):
                    mm = nc.tensor.transpose(ps[:, b, j * P:(j + 1) * P], src[:, j * P:(j + 1) * P], k.ident)
                mm.then_inc(turned, 1)

        def level(tt, m, first, a, b, da, db, op, tmp, step, done):
            w = min(m, tmp.shape[1] // 32)
            for o in range(0, m, w):
                cc, ss = (q[n].unsqueeze(2).to_broadcast([P, 32, w]) for n in step)
                t3 = tmp[:, 0:32 * w].rearrange("p (i t) -> p i t", t=w)
                d = da[:, :, m + o:m + o + w]
                first(tt(d, a[:, :, o:o + w], cc, ALU.mult))
                first(tt(t3, b[:, :, o:o + w], ss, ALU.mult))
                last = tt(d, d, t3, op)
                first(last, done if o + w == m else None)

        @block.vector
        def _(dve):
            v = k.stepper(dve, k.vstep)
            for _ in range(BANKS):
                v(nc.vector.memset(k.spare[:, 0:4], 0.0), k.bank_free)
            del v.n[id(k.bank_free)]
            tt, ts_, stt = nc.vector.tensor_tensor, nc.vector.tensor_scalar, nc.vector.scalar_tensor_tensor
            dve.wait_ge(x_high, 1)
            v(tt(xl, x_raw, xh.bitcast(F32), ALU.subtract), x_low)
            pieces = iter(range(PIECES * AT_A_IN, PIECES * (AT_A_IN + N_A_IN)))

            def low(n):
                for _, c in zip(range(n), pieces):
                    k.low(dve, c)

            dve.wait_ge(dt_ready, 1)
            v(tt(q["lrdt"], q["lr"], q["dt"], ALU.mult))
            v(tt(q["x"], q["li"], q["dt"], ALU.mult))
            v(ts_(q["n"], q["x"], 1.0 / (2 * np.pi), MAGIC, ALU.mult, ALU.add))
            v(ts_(q["n"], q["n"], -MAGIC, None, ALU.add))
            v(stt(out=q["r"], in0=q["n"], scalar=-TWO_PI[0], in1=q["x"], op0=ALU.mult, op1=ALU.add))
            for part in TWO_PI[1:]:
                v(stt(out=q["r"], in0=q["n"], scalar=-part, in1=q["r"], op0=ALU.mult, op1=ALU.add))
            v(ts_(q["r"], q["r"], 3.1415925, -3.1415925, ALU.min, ALU.max))
            v(ts_(q["half"], q["r"], 0.5, None, ALU.mult), angle)
            v(tt(q["inv"], q["lr"], q["lr"], ALU.mult))
            v(tt(q["t0"], q["li"], q["li"], ALU.mult))
            v(tt(q["inv"], q["inv"], q["t0"], ALU.add))
            v(nc.vector.reciprocal(q["inv"], q["inv"]))
            dve.wait_ge(trig, 1)
            low(2)
            v(tt(q["c"], q["sh"], q["sh"], ALU.mult))
            v(ts_(q["c"], q["c"], -2.0, 1.0, ALU.mult, ALU.add))
            v(tt(q["am1"], q["mag"], q["c"], ALU.mult))
            v(ts_(q["am1"], q["am1"], -1.0, None, ALU.add))
            v(tt(q["t2"], q["mag"], q["s"], ALU.mult))
            v(tt(q["t0"], q["am1"], q["lr"], ALU.mult))
            v(tt(q["t1"], q["t2"], q["li"], ALU.mult))
            v(tt(q["cr"], q["t0"], q["t1"], ALU.add))
            v(tt(q["cr"], q["cr"], q["inv"], ALU.mult))
            v(tt(q["t0"], q["t2"], q["lr"], ALU.mult))
            v(tt(q["t1"], q["am1"], q["li"], ALU.mult))
            v(tt(q["ci"], q["t0"], q["t1"], ALU.subtract))
            v(tt(q["ci"], q["ci"], q["inv"], ALU.mult))
            low(4)
            r3 = lambda a: a.rearrange("p (i c) -> p i c", c=32)
            crb, cib = (q[n].unsqueeze(2).to_broadcast([P, 32, 32]) for n in ("cr", "ci"))
            t3 = r3(tmp_v[:, 0:1024])
            v(tt(r3(bbr), r3(bre), crb, ALU.mult))
            v(tt(t3, r3(bim), cib, ALU.mult))
            v(tt(r3(bbr), r3(bbr), t3, ALU.subtract), bbar)
            v(tt(r3(bbi), r3(bim), crb, ALU.mult))
            v(tt(t3, r3(bre), cib, ALU.mult))
            v(tt(r3(bbi), r3(bbi), t3, ALU.add), bbar)
            low(2)
            v(nc.vector.memset(tc3[:, :, 0:1], 1.0))
            v(nc.vector.memset(ts3[:, :, 0:1], 0.0))
            v(nc.vector.tensor_copy(q["cm"], q["c"]))
            v(nc.vector.tensor_copy(q["sm"], q["s"]), step_z)
            now, nxt = ("cm", "sm"), ("cm2", "sm2")
            for n in range(8):
                m = 1 << n
                if n:
                    dve.wait_ge(sin_done, n)
                level(tt, m, v, tc3, ts3, tc3, ts3, ALU.subtract, tmp_v, now, cos_done)
                low(2 if n >= 4 else 1)
                if n < 7:
                    c, s = (q[x] for x in now)
                    v(tt(q["t0"], c, c, ALU.mult))
                    v(tt(q["t1"], s, s, ALU.mult))
                    v(tt(q[nxt[0]], q["t0"], q["t1"], ALU.subtract))
                    v(tt(q["t0"], c, s, ALU.mult))
                    v(ts_(q[nxt[1]], q["t0"], 2.0, None, ALU.mult), step_z)
                    now, nxt = nxt, now
            low(PIECES * N_A_IN)

        @block.gpsimd
        def _(pool):
            g = k.stepper(pool, k.gstep)
            now, nxt = ("cm", "sm"), ("cm2", "sm2")
            for n in range(8):
                pool.wait_ge(step_z, n + 1)
                if n:
                    pool.wait_ge(cos_done, n)
                level(nc.gpsimd.tensor_tensor, 1 << n, g, ts3, tc3, ts3, tc3, ALU.add, tmp_p, now, sin_done)
                now, nxt = nxt, now


def s5_scan(k):
    nc, ps = k.nc, k.ps
    uz, tc, ts = k.at(4096, 4096), k.at(8192, 8192), k.at(16384, 8192)
    q, cre, ncre, ncim, bt_r, bt_i, small = (k.s5[n] for n in ("q", "cre", "ncre", "ncim", "bt_r", "bt_i", "small"))
    gel = k.at(0, 2048)
    ysum = k.at(2048, 2048)
    rooms = [25600 + 512 * i for i in range(4)] + [28672 + 512 * i for i in range(6)] + [35904, 36416]
    buf = lambda n, i: k.at(rooms[2 * n + i % 2], 512)
    BU, Q, G, GG, HC, HS = range(6)
    pair = lambda a: a.rearrange("p (c t) -> p c t", c=2)
    both = lambda a, i: a[:, i * T:(i + 1) * T].unsqueeze(1).to_broadcast([P, 2, T])
    (bu_ready, bu_copied, p_done, q_ready, rotated, scanned, hc_ready, hs_ready, y_mm, y_out, gelu_done) = (
        k.sem(n) for n in ("bu_ready bu_copied bu_by_cos bu_by_sin rotated scanned h_by_cos h_by_sin y_products "
                           "y_summed y_gelu").split())

    with nc.Block() as block:
        @block.tensor
        def _(pe):
            def inputs(i):
                j, s = divmod(i, 4)
                if i >= 2:
                    pe.wait_ge(bu_copied, i - 1)
                u = uz[32 * s:32 * s + 32, j * T:(j + 1) * T]
                for c, bt in ((0, bt_r), (1, bt_i)):
                    mm = nc.tensor.matmul(ps[:, i % 2, c * T:(c + 1) * T], bt[32 * s:32 * s + 32, j * P:(j + 1) * P],
                                          u, start=True, stop=True)
                mm.then_inc(bu_ready, 1)

            def outputs(i):
                j, s = divmod(i, 4)
                pe.wait_ge(hc_ready, i + 1)
                pe.wait_ge(hs_ready, i + 1)
                if s == 0 and j >= 2:
                    pe.wait_ge(y_out, j - 1)
                o = ps[32 * s:32 * s + 32, 2 + j % 2, 0:T]
                hc, hs = pair(buf(HC, i)), pair(buf(HS, i))
                parts = ((cre, hc[:, 0, :]), (ncre, hs[:, 1, :]), (ncim, hs[:, 0, :]), (ncim, hc[:, 1, :]))
                for n, (c, h) in enumerate(parts):
                    mm = nc.tensor.matmul(o, c[:, i * 32:i * 32 + 32], h, start=(n == 0), stop=(n == 3))
                mm.then_inc(y_mm, 1)

            inputs(0)
            for i in range(STILES):
                if i + 1 < STILES:
                    inputs(i + 1)
                outputs(i)

        @block.scalar
        def _(act):
            def gelu(j):
                act.wait_ge(y_out, j + 1)
                nc.scalar.activation(gel[:, j * T:(j + 1) * T], ysum[:, j * T:(j + 1) * T],
                                     ACT.Gelu_apprx_tanh).then_inc(gelu_done, 1)

            for i in range(STILES):
                act.wait_ge(bu_ready, i + 1)
                if i >= 2:
                    act.wait_ge(p_done, i - 1)
                    act.wait_ge(q_ready, i - 1)
                nc.scalar.copy(buf(BU, i), ps[:, i % 2, :]).then_inc(bu_copied, 1)
            for j in range(ECH):
                gelu(j)

        @block.gpsimd
        def _(pool):
            def h_sin(i):
                pool.wait_ge(scanned, i + 1)
                if i >= 2:
                    pool.wait_ge(y_mm, i - 1)
                nc.gpsimd.tensor_tensor(pair(buf(HS, i)), pair(buf(GG, i)), both(ts, i), ALU.mult).then_inc(hs_ready, 1)

            for i in range(STILES):
                pool.wait_ge(bu_copied, i + 1)
                if i >= 2:
                    pool.wait_ge(rotated, i - 1)
                nc.gpsimd.tensor_tensor(pair(buf(Q, i)), pair(buf(BU, i)), both(ts, i), ALU.mult).then_inc(q_ready, 1)
                if i >= 1:
                    h_sin(i - 1)
            h_sin(STILES - 1)

        def skip(v, dve, j):
            dve.wait_ge(y_mm, 4 * j + 4)
            v(nc.vector.scalar_tensor_tensor(out=ysum[:, j * T:(j + 1) * T], in0=uz[:, j * T:(j + 1) * T],
                                             scalar=small[:, j:j + 1], in1=ps[:, 2 + j % 2, 0:T],
                                             op0=ALU.mult, op1=ALU.add), y_out)

        @block.vector
        def _(dve):
            v = k.stepper(dve, k.vstep)
            tt = nc.vector.tensor_tensor
            for i in range(STILES):
                pb, gg, qq = buf(G, 0), buf(GG, i), buf(Q, i)
                gb = buf(G, 1)
                dve.wait_ge(bu_copied, i + 1)
                v(tt(pair(pb), pair(buf(BU, i)), both(tc, i), ALU.mult), p_done)
                dve.wait_ge(q_ready, i + 1)
                v(tt(gb[:, 0:T], pb[:, 0:T], qq[:, T:], ALU.add))
                v(tt(gb[:, T:], pb[:, T:], qq[:, 0:T], ALU.subtract), rotated)
                if i >= 2:
                    dve.wait_ge(hs_ready, i - 1)
                mag = q["mag"][:, i:i + 1].to_broadcast([P, T])
                v(nc.vector.tensor_tensor_scan(gg[:, 0:T], mag, gb[:, 0:T], 0.0, ALU.mult, ALU.add))
                v(nc.vector.tensor_tensor_scan(gg[:, T:], mag, gb[:, T:], 0.0, ALU.mult, ALU.add), scanned)
                if i >= 2:
                    dve.wait_ge(y_mm, i - 1)
                v(tt(pair(buf(HC, i)), pair(gg), both(tc, i), ALU.mult), hc_ready)
                if i % 4 == 0 and i:
                    skip(v, dve, i // 4 - 1)
            skip(v, dve, ECH - 1)


def s5_output(k):
    nc, ps = k.nc, k.ps
    gel, uz, small = k.at(0, 2048), k.at(4096, 4096), k.s5["small"]
    z = uz[:, 2048:]
    sig, yy, sz = k.at(25600, 2048), k.at(27648, 2048), k.at(29696, 2048)
    gel_parts, yy_parts = k.split_x(35904, 0, 2048), k.split_x(36928, 2048, 2048)
    x, dst = k.at(8192, 4096), k.at(12288, 4096)
    xs, z_done, g_high, g_low, y_done, y_high, y_low, one = (k.sem(n) for n in (
        "x_rows z_silu g_high g_low y_gated y_high y_low glu_piece").split())

    def pieces(pe, first, n, parts, glu):
        for t in range(first, first + n):
            pe.wait_ge(k.bank_free, t + 1)
            for part in range(PIECES):
                piece = PIECES * t + part
                pe.wait_ge(k.low_done, piece + 1)
                for kk in range(ECH // PIECES):
                    c = part * (ECH // PIECES) + kk
                    for sub in range(4 if glu else 2):
                        if glu:
                            out = ps[:, t % BANKS + 3 * (sub // 2), (sub % 2) * T:(sub % 2) * T + T]
                            pairs = channel_products(k.parts(piece % SLOTS), parts,
                                                     slice(kk * 512 + sub * P, kk * 512 + sub * P + P),
                                                     slice(c * T, (c + 1) * T))
                        else:
                            out = ps[:, t % BANKS + 3 * sub, :]
                            pairs = token_products(k.parts(piece % SLOTS), parts, slice(kk * 512, (kk + 1) * 512),
                                                   slice(c * T + sub * P, c * T + sub * P + P))
                        for i, (a, b) in enumerate(pairs):
                            mm = nc.tensor.matmul(out, a, b, start=(c == 0 and i == 0 and (not glu or sub % 2 == 0)),
                                                  stop=(c == ECH - 1 and i == 2 and (not glu or sub % 2 == 1)),
                                                  skip_group_check=True)
                mm.then_inc(k.multiplied, 1)

    with nc.Block() as block:
        @block.sync
        def _(sp):
            sp.dma_start(x, k.ins["x_rows"]).then_inc(xs, 16)
            k.stream(sp, AT_KV)

        @block.tensor
        def _(pe):
            pe.wait_ge(g_low, 1)
            pieces(pe, AT_GLU, N_GLU, gel_parts, True)
            pe.wait_ge(y_low, 1)
            pieces(pe, AT_A_OUT, N_A_OUT, yy_parts, False)

        @block.scalar
        def _(act):
            a = k.stepper(act, k.astep)
            a(nc.scalar.copy(gel_parts[0], gel), g_high)
            for c in range(PIECES * AT_GLU, PIECES * (AT_GLU + 1)):
                k.high(act, c)
            a(nc.scalar.activation(sz, z, ACT.Silu), z_done)
            for n in range(N_GLU):
                t = AT_GLU + n
                for c in range(PIECES * (t + 1), PIECES * (t + 2)):
                    k.high(act, c)
                act.wait_ge(k.multiplied, PIECES * (t + 1))
                for sub in range(4):
                    j = 4 * n + sub
                    last = nc.scalar.activation(sig[:, j * T:(j + 1) * T],
                                                ps[:, t % BANKS + 3 * (sub // 2), (sub % 2) * T:(sub % 2) * T + T],
                                                ACT.Sigmoid, bias=small[:, 8 + j:9 + j])
                    last.then_inc(k.bank_free if sub == 3 else one, 1)
            act.wait_ge(k.bank_free, AT_GLU + N_GLU + BANKS)
            act.wait_ge(y_done, 1)
            a(nc.scalar.copy(yy_parts[0], yy), y_high)
            for c in range(PIECES * (AT_A_OUT + 1), PIECES * (AT_A_OUT + N_A_OUT)):
                k.high(act, c)

        @block.vector
        def _(dve):
            v = k.stepper(dve, k.vstep)
            dve.wait_ge(g_high, 1)
            v(nc.vector.tensor_tensor(gel_parts[1], gel, gel_parts[0].bitcast(F32), ALU.subtract), g_low)
            for c in range(PIECES * AT_GLU, PIECES * (AT_GLU + N_GLU)):
                k.low(dve, c)
            dve.wait_ge(z_done, 1)
            v(nc.vector.tensor_tensor(sz, sz, gel, ALU.mult))
            for c in range(PIECES * AT_A_OUT, PIECES * (AT_A_OUT + 1)):
                k.low(dve, c)
            dve.wait_ge(k.bank_free, AT_GLU + N_GLU + BANKS)
            v(nc.vector.tensor_tensor(yy, sig, sz, ALU.mult), y_done)
            dve.wait_ge(y_high, 1)
            v(nc.vector.tensor_tensor(yy_parts[1], yy, yy_parts[0].bitcast(F32), ALU.subtract), y_low)
            dve.wait_ge(xs, 16)
            for n in range(N_A_OUT):
                t = AT_A_OUT + n
                if n < N_A_OUT - 1:
                    for c in range(PIECES * (t + 1), PIECES * (t + 2)):
                        k.low(dve, c)
                dve.wait_ge(k.multiplied, PIECES * (t + 1))
                for tt in range(TT):
                    cols = slice(tt * D + n * 512, tt * D + n * 512 + 512)
                    last = nc.vector.scalar_tensor_tensor(out=dst[:, cols], in0=x[:, cols], scalar=ALPHA,
                                                          in1=ps[:, t % BANKS + 3 * tt, :], op0=ALU.mult, op1=ALU.add)
                    if tt == 0:
                        v(last)
                    else:
                        last.then_inc(k.bank_free, 1)
            dve.wait_ge(k.bank_free, AT_A_OUT + N_A_OUT + BANKS)


H1, KV, QT, Z, GATE, Y, KC_T, VC, W_GATE, ATT = 0, 4096, 10240, 14336, 26624, 26752, 30848, 30976, 31488, 32256
H1_LOW = Y


def shared_keys_values(k):
    nc, ps = k.nc, k.ps
    hT, kv = k.split_x(H1_LOW), k.at(KV, 6144)
    with nc.Block() as block:
        @block.sync
        def _(sp):
            k.stream(sp, AT_B_IN)

        @block.tensor
        def _(pe):
            for first, n, kind in ((0, 6, "channel"), (6, 2, "token"), (8, 2, "channel"), (10, 2, "token")):
                k.multiply(pe, AT_KV + first, n, hT, kind)

        @block.scalar
        def _(act):
            k.split_and_drain(act, AT_KV, N_KV, k.high,
                              lambda s, j: nc.scalar.copy(kv[:, bass.ds(j * BANK, BANK)], ps[:, s, :]))

        @block.vector
        def _(dve):
            k.split_and_drain(dve, AT_KV, N_KV, k.low)


def compress(k):
    nc, ps = k.nc, k.ps
    kv = k.at(KV, 6144)
    w1 = [k.at(Z, 4096), k.at(Z + 4096, 4096)]
    w2 = [k.at(Z + 8192, P), k.at(Z + 8192 + P, P)]
    pos = [k.at(Z + 8192 + 2 * P, 32), k.at(Z + 8224 + 2 * P, 32)]
    hid = [k.at(Z + 8192 + 3 * P, 64), k.at(Z + 8256 + 3 * P, 64)]
    bias = k.at(Z + 8192 + 4 * P, 8)
    kcT, vc = k.at(KC_T, KVH * NCMP), k.at(VC, KVH * HD)
    w_in, pos_sum, pos_out, hid_sum, hid_out, out_sum, c_out = (
        k.sem(n) for n in "cmp_weights pos_sum pos_copied hidden_sum hidden_gelu cmp_sum cmp_copied".split())
    n = KVH * NCMP
    with nc.Block() as block:
        @block.sync
        def _(sp):
            for i, kv_name in enumerate("kv"):
                sp.dma_start(w1[i], k.ins[f"cmp_w1_{kv_name}"]).then_inc(w_in, 16)
                sp.dma_start(w2[i], k.ins[f"cmp_w2_{kv_name}"]).then_inc(w_in, 16)
                sp.dma_start(pos[i], k.ins[f"cmp_pos_{kv_name}"]).then_inc(w_in, 16)

        @block.tensor
        def _(pe):
            pe.wait_ge(w_in, 96)
            for i in range(2):
                src = kv[:, 2 * i * BANK:(2 * i + 2) * BANK].rearrange("p (h t) -> p h t", t=T)
                for l in range(CBLOCK):
                    w = w1[i][:, l * P:(l + 1) * P]
                    mm = nc.tensor.matmul(ps[:, 2 + i, 0:1], w, pos[i][:, l:l + 1], start=(l == 0), stop=(l == CBLOCK - 1))
                mm.then_inc(pos_sum, 1)
                for l in range(CBLOCK):
                    w = w1[i][:, l * P:(l + 1) * P]
                    mm = nc.tensor.matmul(ps[:, i, 0:n].rearrange("p (h b) -> p h b", b=NCMP), w,
                                          src[:, :, l:l + CSTRIDE * (NCMP - 1) + 1:CSTRIDE],
                                          start=(l == 0), stop=(l == CBLOCK - 1))
                mm.then_inc(hid_sum, 1)
            pe.wait_ge(hid_out, 2)
            nc.tensor.matmul(ps[:, 4, 0:n], w2[0], hid[0][:, 0:n], start=True, stop=True).then_inc(out_sum, 1)
            for h in range(KVH):
                mm = nc.tensor.matmul(ps[0:NCMP, 5, h * HD:(h + 1) * HD], hid[1][:, h * NCMP:(h + 1) * NCMP], w2[1],
                                      start=True, stop=True)
            mm.then_inc(out_sum, 1)

        @block.vector
        def _(dve):
            for i in range(2):
                dve.wait_ge(pos_sum, i + 1)
                nc.vector.tensor_copy(bias[:, i:i + 1], ps[:, 2 + i, 0:1]).then_inc(pos_out, 1)
            dve.wait_ge(out_sum, 1)
            nc.vector.tensor_copy(kcT, ps[:, 4, 0:n]).then_inc(c_out, 1)
            dve.wait_ge(out_sum, 2)
            nc.vector.tensor_copy(vc[0:NCMP, :], ps[0:NCMP, 5, :]).then_inc(c_out, 1)

        @block.scalar
        def _(act):
            for i in range(2):
                act.wait_ge(pos_out, i + 1)
                act.wait_ge(hid_sum, i + 1)
                nc.scalar.activation(hid[i][:, 0:n], ps[:, i, 0:n], ACT.Gelu_apprx_tanh,
                                     bias=bias[:, i:i + 1]).then_inc(hid_out, 1)


def small_product(k, pe, x, parts, n, width, out):
    for tt in range(TT):
        for c in range(KC):
            pairs = token_products(parts, x, slice(c * n, (c + 1) * n), slice(c * T + tt * P, c * T + tt * P + P))
            for i, (a, b) in enumerate(pairs):
                mm = k.nc.tensor.matmul(out[:, tt * width:tt * width + n], a, b, start=(c == 0 and i == 0),
                                        stop=(c == KC - 1 and i == 2))
    return mm


def attention_inputs(k):
    nc, ps = k.nc, k.ps
    hT, q, z = k.split_x(H1_LOW), k.at(QT, 4096), k.at(Z, 12288)
    gate, w = k.at(GATE, TT * 48), k.at(W_GATE, KC * 48)
    parts = k.split_small(ATT, KC * 48)
    w_in, w_high, w_low, g_sum = k.sem("gate_weights"), k.sem("gate_w_high"), k.sem("gate_w_low"), k.sem("gate_sum")
    with nc.Block() as block:
        @block.sync
        def _(sp):
            sp.dma_start(w, k.ins["w_gate"]).then_inc(w_in, 16)
            k.stream(sp, AT_B_OUT)

        @block.tensor
        def _(pe):
            k.multiply(pe, AT_B_IN, 8, hT, "channel")
            k.multiply(pe, AT_B_IN + 8, 24, hT, "token")
            pe.wait_ge(w_low, 1)
            small_product(k, pe, hT, parts, 48, 64, ps[:, 6, :]).then_inc(g_sum, 1)

        @block.vector
        def _(dve):
            k.split_and_drain(dve, AT_B_IN, N_B_IN, k.low)
            dve.wait_ge(w_high, 1)
            nc.vector.tensor_tensor(parts[1], w, parts[0].bitcast(F32), ALU.subtract).then_inc(w_low, 1)

        @block.scalar
        def _(act):
            k.split_and_drain(act, AT_B_IN, 8, k.high,
                              lambda s, j: nc.scalar.copy(q[:, bass.ds(j * BANK, BANK)], ps[:, s, :]))
            k.split_and_drain(act, AT_B_IN + 8, 24, k.high,
                              lambda s, j: nc.scalar.activation(z[:, bass.ds(j * BANK, BANK)], ps[:, s, :], ACT.Silu))
            act.wait_ge(w_in, 16)
            nc.scalar.copy(parts[0], w).then_inc(w_high, 1)
            act.wait_ge(g_sum, 1)
            nc.scalar.activation(gate.rearrange("p (a n) -> p a n", a=TT),
                                 ps[:, 6, 0:TT * 64].rearrange("p (a n) -> p a n", a=TT)[:, :, 0:48],
                                 ACT.Sigmoid).then_inc(g_sum, 1)
            act.wait_ge(g_sum, 2)


def attention(k):
    nc, ps = k.nc, k.ps
    kv, q, z, gate, y = k.at(KV, 6144), k.at(QT, 4096), k.at(Z, 12288), k.at(GATE, TT * 48), k.at(Y, 4096)
    kcT, vc = k.at(KC_T, KVH * NCMP), k.at(VC, KVH * HD)
    o = ATT
    tri = k.at(o, P)
    cadd, cmul = k.at(o + P, TT * 16), k.at(o + P + 32, TT * 16)
    ce = k.at(o + 256, TT * 240)
    cs = k.at(o + 736, 160)
    prob = [k.at(o + 1024, 512), k.at(o + 1536, 512)]
    probT = [k.at(o + 2048, 512), k.at(o + 2560, 512)]
    cT = [k.at(o + 3072, P), k.at(o + 3200, P)]
    oz = k.at(o + 3328, 384)
    st = [k.at(o + 3712 + 16 * i, 16) for i in range(2)]
    (masks, c_scores, c_raised, c_exp, c_norm, s_ready, m_ready, e_ready, turned, c_turned, pt_ready, ct_ready, o_ready,
     o_read) = (k.sem("att_" + n) for n in (
         "masks cmp_scores cmp_raised cmp_exp cmp_norm scores_ready max_ready probs_ready turned cmp_turned "
         "turned_copied cmp_copied out_ready out_read").split())
    steps = [(tt, h) for tt in range(TT) for h in range(HEADS)]
    n_steps = len(steps)

    def keys(tile, g, n):
        return kv[:, tile * BANK + g * T:tile * BANK + g * T + n]

    def values(tile, g, kb):
        at = (tile + g // 2) * BANK + kb * 256 + (g % 2) * HD
        return kv[:, at:at + HD]

    with nc.Block() as block:
        @block.sync
        def _(sp):
            sp.dma_start(k.at(o, 192), k.ins["att_masks"]).then_inc(masks, 16)

        @block.tensor
        def _(pe):
            def qh(i):
                tt, h = steps[i]
                return q[:, h * T + tt * P:h * T + tt * P + P]

            def scores(i):
                tt, h = steps[i]
                n = P * (tt + 1)
                if i >= 2:
                    pe.wait_ge(e_ready, i - 1)
                for b, tile in enumerate((4, 8)):
                    out = ps[:, i % 2, b * T:b * T + n]
                    nc.tensor.matmul(out, qh(i), keys(tile, h // 4, n), start=True, stop=False)
                    mm = nc.tensor.matmul(ps[:, i % 2, b * T + n - P:b * T + n], k.ident, tri, start=False, stop=True)
                mm.then_inc(s_ready, 1)

            def turn(i):
                tt, h = steps[i]
                pe.wait_ge(e_ready, i + 1)
                if i >= 2:
                    pe.wait_ge(pt_ready, i - 1)
                    pe.wait_ge(ct_ready, i - 1)
                nc.tensor.transpose(ps[0:NCMP, 6 + i % 2, 0:P], ce[:, tt * 240 + h * 15:tt * 240 + h * 15 + 15],
                                    k.ident).then_inc(c_turned, 1)
                for b in range(2):
                    for kb in range(tt + 1):
                        n = b * (tt + 1) + kb
                        mm = nc.tensor.transpose(ps[:, 2 + i % 2, n * P:(n + 1) * P],
                                                 prob[i % 2][:, b * T + kb * P:b * T + kb * P + P], k.ident)
                mm.then_inc(turned, 1)

            def outputs(i):
                tt, h = steps[i]
                g = h // 4
                pe.wait_ge(ct_ready, i + 1)
                pe.wait_ge(pt_ready, i + 1)
                if i >= 2:
                    pe.wait_ge(o_read, i - 1)
                bank = ps[:, 4 + i % 2, :]
                nc.tensor.matmul(bank[:, 0:HD], cT[i % 2][0:NCMP, :], vc[0:NCMP, g * HD:(g + 1) * HD],
                                 start=True, stop=True)
                for b, tile in enumerate((6, 10)):
                    for kb in range(tt + 1):
                        n = b * (tt + 1) + kb
                        mm = nc.tensor.matmul(bank[:, (b + 1) * HD:(b + 2) * HD], probT[i % 2][:, n * P:(n + 1) * P],
                                              values(tile, g, kb), start=(kb == 0), stop=(kb == tt))
                mm.then_inc(o_ready, 1)

            for i in range(n_steps):
                tt, h = steps[i]
                mm = nc.tensor.matmul(ps[:, 6 + tt, h * 15:h * 15 + 15], qh(i),
                                      kcT[:, (h // 4) * NCMP:(h // 4 + 1) * NCMP], start=True, stop=True)
                if h == HEADS - 1:
                    mm.then_inc(c_scores, 1)
            pe.wait_ge(masks, 16)
            for i in range(n_steps + 2):
                if i < n_steps:
                    scores(i)
                if 1 <= i <= n_steps:
                    if i == 1:
                        pe.wait_ge(c_norm, 2)
                    turn(i - 1)
                if i >= 2:
                    outputs(i - 2)

        @block.scalar
        def _(act):
            def exps(i):
                tt, h = steps[i]
                n = P * (tt + 1)
                act.wait_ge(m_ready, i + 1)
                if i >= 2:
                    act.wait_ge(turned, i - 1)
                    act.wait_ge(o_read, i - 1)
                for b in range(2):
                    a(nc.scalar.activation(prob[i % 2][:, b * T:b * T + n], ps[:, i % 2, b * T:b * T + n], ACT.Exp,
                                           bias=st[i % 2][:, 2 + b:3 + b], scale=SCALE,
                                           accum_out=st[i % 2][:, 4 + b:5 + b]), e_ready if b else None)

            def copy(i):
                tt, h = steps[i]
                act.wait_ge(turned, i + 1)
                if i >= 2:
                    act.wait_ge(o_ready, i - 1)
                n = 2 * (tt + 1) * P
                nc.scalar.copy(probT[i % 2][:, 0:n], ps[:, 2 + i % 2, 0:n]).then_inc(pt_ready, 1)

            a = k.stepper(act, k.astep)
            for tt in range(TT):
                act.wait_ge(c_raised, tt + 1)
                nc.scalar.activation(ce[:, tt * 240:(tt + 1) * 240], ce[:, tt * 240:(tt + 1) * 240], ACT.Exp,
                                     scale=SCALE).then_inc(c_exp, 1)
            for i in range(n_steps + 1):
                if i < n_steps:
                    exps(i)
                if i >= 1:
                    copy(i - 1)

        @block.vector
        def _(dve):
            v = k.stepper(dve, k.vstep)
            tt_ = nc.vector.tensor_tensor
            dve.wait_ge(masks, 16)
            for tt in range(TT):
                c3 = ce[:, tt * 240:(tt + 1) * 240].rearrange("p (h n) -> p h n", n=NCMP)
                mask = [m[:, tt * 16:tt * 16 + 15].unsqueeze(1).to_broadcast([P, HEADS, NCMP]) for m in (cadd, cmul)]
                mx = cs[:, 64 + tt * 16:80 + tt * 16]
                dve.wait_ge(c_scores, tt + 1)
                v(tt_(c3, ps[:, 6 + tt, 0:240].rearrange("p (h n) -> p h n", n=NCMP), mask[0], ALU.add))
                v(nc.vector.tensor_reduce(mx, c3, AX.X, ALU.max))
                v(tt_(c3, c3, mx.unsqueeze(2).to_broadcast([P, HEADS, NCMP]), ALU.subtract), c_raised)
                dve.wait_ge(c_exp, tt + 1)
                v(tt_(c3, c3, mask[1], ALU.mult))
                v(nc.vector.tensor_reduce(mx, c3, AX.X, ALU.add))
                v(nc.vector.tensor_scalar(mx, mx, 1e-30, None, ALU.max))
                v(nc.vector.reciprocal(mx, mx))
                v(tt_(cs[:, tt * 16:tt * 16 + 16], mx, gate[:, tt * 48:tt * 48 + 16], ALU.mult), c_norm)

            def maxes(i):
                tt, h = steps[i]
                n = P * (tt + 1)
                dve.wait_ge(s_ready, i + 1)
                if i >= 2:
                    dve.wait_ge(e_ready, i - 1)
                v(nc.vector.tensor_reduce(st[i % 2][:, 0:2], ps[:, i % 2, :].rearrange("p (b n) -> p b n", b=2)[:, :, 0:n],
                                          AX.X, ALU.max))
                v(nc.vector.tensor_scalar(st[i % 2][:, 2:4], st[i % 2][:, 0:2], -SCALE, None, ALU.mult), m_ready)

            def copy(i):
                dve.wait_ge(c_turned, i + 1)
                if i >= 2:
                    dve.wait_ge(o_ready, i - 1)
                v(nc.vector.tensor_copy(cT[i % 2][0:NCMP, :], ps[0:NCMP, 6 + i % 2, 0:P]), ct_ready)

            def combine(i):
                tt, h = steps[i]
                s = st[i % 2]
                dve.wait_ge(o_ready, i + 1)
                v(nc.vector.reciprocal(s[:, 6:8], s[:, 4:6]))
                v(tt_(s[:, 8:10], s[:, 6:8], gate[:, tt * 48 + 16 + h:tt * 48 + 48:16], ALU.mult))
                zs = z.rearrange("p (b w) -> p b w", b=3)[:, :, (h // 2) * 512 + tt * 256 + (h % 2) * HD:
                                                          (h // 2) * 512 + tt * 256 + (h % 2) * HD + HD]
                v(tt_(oz.rearrange("p (b d) -> p b d", b=3),
                      ps[:, 4 + i % 2, 0:384].rearrange("p (b d) -> p b d", b=3), zs, ALU.mult), o_read)
                dst = y[:, tt * D + h * HD:tt * D + h * HD + HD]
                c = cs[:, tt * 16 + h:tt * 16 + h + 1]
                v(nc.vector.tensor_scalar(dst, oz[:, 0:HD], c, None, ALU.mult))
                for b in range(2):
                    v(nc.vector.scalar_tensor_tensor(out=dst, in0=oz[:, (b + 1) * HD:(b + 2) * HD],
                                                     scalar=s[:, 8 + b:9 + b], in1=dst, op0=ALU.mult, op1=ALU.add))

            for i in range(n_steps + 2):
                if i < n_steps:
                    maxes(i)
                if 1 <= i <= n_steps:
                    copy(i - 1)
                if i >= 2:
                    combine(i - 2)


def first_block(k):
    s5_inputs_and_tables(k)
    s5_scan(k)
    s5_output(k)
    h = k.at(12288, 4096)
    k.layer_norm(h, k.at(H1, 4096), 0, k.at(16384, 2048), k.at(18432, 2048), k.at(20480, 64),
                 k.split_x(H1_LOW), AT_KV)
    shared_keys_values(k)
    compress(k)
    attention_inputs(k)
    attention(k)
    yT, pre = k.split_x(Z + 8192), k.at(Z + 4096, 4096)
    k.transposes(k.at(Y, 4096), yT, AT_B_OUT)
    k.project_residual(AT_B_OUT, N_B_OUT, yT, k.at(H1, 4096), ALPHA, pre, AT_IN2)
    return pre


H2, PR, BA, FREE = 0, 8192, 22528, 22560
W_BETA = FREE + 4096
MIX = 4096
XN_LOW, MIX_LOW = FREE + 2048, 32768
PR_AQ, PR_AF, PR_AI, PR_AG, PR_BQ, PR_BZ = (PR + 2048 * n for n in (0, 1, 2, 3, 4, 6))
BDK = 128


def token_head(k, base, tt, h):
    return k.at(base + (h // 2) * BANK + tt * 256 + (h % 2) * P, P)


def second_inputs(k):
    nc, ps = k.nc, k.ps
    normed = k.sem("xn_ready")
    xT = k.split_x(XN_LOW)
    k.transposes(k.at(8192, 4096), xT, AT_IN2, lambda block: (
        k.rms_scale(block, k.at(H2, 4096), "attn_norm_g_2", k.at(12288, 2048), k.at(14336, 16), k.at(8192, 4096),
                    "in2", normed) or [(normed, TT)]))
    pr, w, ba = k.at(PR, 14336), k.at(W_BETA, KC * 16), k.at(BA, 32)
    parts = k.split_small(FREE, KC * 16)
    w_in, w_high, w_low, b_sum = k.sem("beta_weights"), k.sem("beta_w_high"), k.sem("beta_w_low"), k.sem("beta_sum")
    with nc.Block() as block:
        @block.sync
        def _(sp):
            sp.dma_start(w, k.ins["w_beta"]).then_inc(w_in, 16)
            k.stream(sp, AT_OUT2)

        @block.tensor
        def _(pe):
            for first, n, kind in ((0, 8, "channel"), (8, 8, "token"), (16, 8, "channel"), (24, 4, "token")):
                k.multiply(pe, AT_IN2 + first, n, xT, kind)
            pe.wait_ge(w_low, 1)
            small_product(k, pe, xT, parts, 16, 16, ps[:, 6, :]).then_inc(b_sum, 1)

        @block.vector
        def _(dve):
            k.split_and_drain(dve, AT_IN2, N_IN2, k.low)
            dve.wait_ge(w_high, 1)
            nc.vector.tensor_tensor(parts[1], w, parts[0].bitcast(F32), ALU.subtract).then_inc(w_low, 1)

        @block.scalar
        def _(act):
            k.split_and_drain(act, AT_IN2, N_IN2, k.high,
                              lambda s, j: nc.scalar.copy(pr[:, bass.ds(j * BANK, BANK)], ps[:, s, :]))
            act.wait_ge(w_in, 16)
            nc.scalar.copy(parts[0], w).then_inc(w_high, 1)
            act.wait_ge(b_sum, 1)
            nc.scalar.copy(ba, ps[:, 6, 0:32]).then_inc(b_sum, 1)
            act.wait_ge(b_sum, 2)


def hgrn(k):
    nc, ps = k.nc, k.ps
    n_ch = T // CH
    aq, af = k.at(PR_AQ, 2048), k.at(PR_AF, 2048)
    qa, ka, b, ktok = (k.at(FREE + 2048 * i, 2048) for i in range(4))
    st = [k.at(FREE + 8192 + 1024 * i, 1024) for i in range(2)]
    att = [k.at(FREE + 10240 + 256 * i, 256) for i in range(2)]
    fac = k.at(FREE + 10752, 64)
    lg = k.at(FREE + 10816, 64)
    tri = k.at(FREE + 10880, CH)
    en, reset = k.at(FREE + 10912, 2048), k.at(FREE + 12960, 2048)
    mix = k.at(MIX, 4096)
    lb, oml = lg[:, 48:56], lg[:, 56:64]
    (logits, lb_exp, sig, f_ready, logged, centred, exps, scaled, turned, kt_ready, att_ready, att_masked, ds_ready,
     o_ready, s_ready, fac_in) = (k.sem("hg_" + n) for n in (
         "logits lb_ready sigmoids f_ready log_f centred exps scaled turned k_tokens att_ready att_masked ds_ready "
         "out_ready state_ready fac_in").split())
    chunks = lambda a: a.rearrange("p (n c) -> p n c", c=CH)

    with nc.Block() as block:
        @block.sync
        def _(sp):
            sp.dma_start(lg[:, 0:16], k.ins["hgrn_lb"]).then_inc(logits, 16)
            sp.dma_start(tri, k.ins["masks2"][:, 4 * P:4 * P + CH]).then_inc(logits, 16)

        @block.scalar
        def _(act):
            a = k.stepper(act, k.astep)
            a(nc.scalar.activation(b, af, ACT.Sigmoid), sig)
            a(nc.scalar.activation(ka, af, ACT.Sigmoid, scale=-1.0), sig)
            act.wait_ge(lb_exp, 1)
            nc.scalar.activation(lg[:, 24:40], lg[:, 24:40], ACT.Exp).then_inc(fac_in, 1)
            act.wait_ge(f_ready, 1)
            nc.scalar.activation(b, b, ACT.Ln).then_inc(logged, 1)
            act.wait_ge(centred, 1)
            a(nc.scalar.activation(qa, b, ACT.Exp), exps)
            act.wait_ge(centred, 2)
            a(nc.scalar.activation(en, b, ACT.Exp, scale=-1.0), exps)
            a(nc.scalar.activation(fac, fac, ACT.Exp), exps)
            for n in range(4):
                act.wait_ge(turned, n + 1)
                nc.scalar.copy(ktok[:, n * BANK:(n + 1) * BANK], ps[:, 4 + n, :]).then_inc(kt_ready, 1)
            for tt in range(TT):
                act.wait_ge(o_ready, 4 * (tt + 1))
                for n in range(2):
                    a(nc.scalar.copy(mix[:, tt * D + n * BANK:tt * D + (n + 1) * BANK],
                                     ps[:, (2 if tt == 0 else 6) + n, :]))

        @block.vector
        def _(dve):
            v = k.stepper(dve, k.vstep)
            tt_, ts_ = nc.vector.tensor_tensor, nc.vector.tensor_scalar
            dve.wait_ge(logits, 32)
            v(tt_(lg[:, 16:24], lg[:, 0:8], lg[:, 8:16], ALU.max))
            v(tt_(lg[:, 24:32], lg[:, 0:8], lg[:, 16:24], ALU.subtract))
            v(tt_(lg[:, 32:40], lg[:, 8:16], lg[:, 16:24], ALU.subtract), lb_exp)
            v(nc.vector.memset(reset, 1.0))
            v(nc.vector.memset(chunks(reset)[:, :, 0:1], 0.0))
            dve.wait_ge(fac_in, 1)
            v(tt_(lg[:, 40:48], lg[:, 24:32], lg[:, 32:40], ALU.add))
            v(nc.vector.reciprocal(lg[:, 40:48], lg[:, 40:48]))
            v(tt_(lb, lg[:, 24:32], lg[:, 40:48], ALU.mult))
            v(ts_(oml, lb, -1.0, 1.0, ALU.mult, ALU.add))
            dve.wait_ge(sig, 2)
            for h in range(AH):
                bh = b[:, h * T:(h + 1) * T]
                v(ts_(bh, bh, oml[:, h:h + 1], lb[:, h:h + 1], ALU.mult, ALU.add), f_ready if h == AH - 1 else None)
            dve.wait_ge(logged, 1)
            v(nc.vector.tensor_tensor_scan(en, reset, b, 0.0, ALU.mult, ALU.add))
            e3 = chunks(en)
            v(tt_(chunks(b), e3, e3[:, :, CH // 2 - 1:CH // 2].to_broadcast([P, AH * n_ch, CH]), ALU.subtract), centred)
            mid, last = e3[:, :, CH // 2 - 1:CH // 2], e3[:, :, CH - 1:CH]
            f3 = fac.unsqueeze(2)
            v(tt_(f3, last, mid, ALU.subtract))
            mid4 = en.rearrange("p (h n c) -> p h n c", h=AH, c=CH)[:, :, 1:, CH // 2 - 1]
            f4 = fac.rearrange("p (h n) -> p h n", h=AH)[:, :, 0:n_ch - 1]
            v(tt_(f4, f4, mid4, ALU.add), centred)
            dve.wait_ge(exps, 2)
            v(tt_(qa, qa, aq, ALU.mult), scaled)
            for h in range(AH):
                kh = ka[:, h * T:(h + 1) * T]
                v(nc.vector.scalar_tensor_tensor(out=kh, in0=kh, scalar=oml[:, h:h + 1], in1=en[:, h * T:(h + 1) * T],
                                                 op0=ALU.mult, op1=ALU.mult), scaled)
            dve.wait_ge(exps, 3)
            for cc in range(n_ch):
                if cc % NCH == 0:
                    tt = cc // NCH
                    dve.wait_ge(att_ready, tt + 1)
                    v(tt_(att[tt].rearrange("p (h c) -> p h c", c=CH), ps[:, tt, 0:256].rearrange("p (h c) -> p h c", c=CH),
                          tri.unsqueeze(1).to_broadcast([P, AH, CH]), ALU.mult), att_masked)
                if cc == n_ch - 1:
                    break
                new = st[(cc + 1) % 2]
                d3 = ps[:, 4:6, :].rearrange("p b n -> p (b n)").rearrange("p (h d) -> p h d", h=AH)
                n3 = new.rearrange("p (h d) -> p h d", h=AH)
                f = fac.rearrange("p (h n) -> p h n", h=AH)[:, :, cc:cc + 1].to_broadcast([P, AH, P])
                dve.wait_ge(ds_ready, cc + 1)
                if cc == 0:
                    v(tt_(n3, d3, f, ALU.mult), s_ready)
                else:
                    if cc >= 2:
                        dve.wait_ge(o_ready, cc)
                    v(tt_(n3, st[cc % 2].rearrange("p (h d) -> p h d", h=AH), d3, ALU.add))
                    v(tt_(n3, n3, f, ALU.mult), s_ready)

        @block.tensor
        def _(pe):
            pe.wait_ge(scaled, 1 + AH)
            for tt in range(TT):
                for c in range(NCH):
                    for h in range(AH):
                        at = h * T + tt * P + c * CH
                        mm = nc.tensor.matmul(ps[32 * c:32 * c + 32, tt, h * CH:(h + 1) * CH], ka[:, at:at + CH],
                                              qa[:, at:at + CH], start=True, stop=True)
                mm.then_inc(att_ready, 1)
            for n in range(4):
                for j in range(4):
                    tt, h = n // 2, 4 * (n % 2) + j
                    mm = nc.tensor.transpose(ps[:, 4 + n, j * P:(j + 1) * P], ka[:, h * T + tt * P:h * T + tt * P + P],
                                             k.ident)
                mm.then_inc(turned, 1)
            pe.wait_ge(kt_ready, 4)
            for cc in range(n_ch):
                tt, c = divmod(cc, NCH)
                rows = slice(32 * c, 32 * c + 32)
                if cc < n_ch - 1:
                    if cc:
                        pe.wait_ge(s_ready, cc)
                    for h in range(AH):
                        mm = nc.tensor.matmul(ps[:, 4 + h // 4, (h % 4) * P:(h % 4) * P + P],
                                              ktok[rows, tt * 1024 + h * P:tt * 1024 + h * P + P],
                                              token_head(k, PR_AI, tt, h)[rows], start=True, stop=True)
                    mm.then_inc(ds_ready, 1)
                pe.wait_ge(att_masked, tt + 1)
                if cc:
                    pe.wait_ge(s_ready, cc)
                for h in range(AH):
                    out = ps[rows, (2 if tt == 0 else 6) + h // 4, (h % 4) * P:(h % 4) * P + P]
                    mm = nc.tensor.matmul(out, att[tt][rows, h * CH:(h + 1) * CH], token_head(k, PR_AI, tt, h)[rows],
                                          start=True, stop=(cc == 0))
                    if cc:
                        at = h * T + cc * CH
                        mm = nc.tensor.matmul(out, qa[:, at:at + CH], st[cc % 2][:, h * P:(h + 1) * P],
                                              start=False, stop=True)
                mm.then_inc(o_ready, 1)


QKV, TOK = FREE, FREE + 4096
QKT, LM, LTM, NM = PR_AQ, PR_AF, PR_AI, FREE + 8192
TM, UM, QM, CM = FREE, FREE + 2048, FREE + 10240, FREE + 12288
AQ = PR_BQ + 2048
GDN_SMALL = FREE + 14336
MASKS = FREE + 14912
XT = PR_BQ
TRIU, TRIU_S, TRIL, TRIL_S, LEVELS = 0, P, 2 * P, 3 * P, 4 * P


def gdn_convolve(k):
    nc, ps = k.nc, k.ps
    src, qkv, tok, cw = k.at(PR_BQ, 4096), k.at(QKV, 4096), k.at(TOK, 4096), k.at(GDN_SMALL, 64)
    w_in, conv, act_done, turned, copied = (k.sem("cv_" + n) for n in "weights convolved silu turned copied".split())
    with nc.Block() as block:
        @block.sync
        def _(sp):
            sp.dma_start(cw, k.ins["conv_w"]).then_inc(w_in, 16)
            sp.dma_start(k.at(MASKS, 4 * P), k.ins["masks2"][:, 0:4 * P]).then_inc(w_in, 16)
            sp.dma_start(k.at(MASKS + 4 * P, 7 * P), k.ins["masks2"][:, 4 * P + CH:]).then_inc(w_in, 16)

        @block.vector
        def _(dve):
            v = k.stepper(dve, k.vstep)
            dve.wait_ge(w_in, 48)
            for j in range(16):
                x, y = src[:, j * T:(j + 1) * T], qkv[:, j * T:(j + 1) * T]
                w = [cw[:, 4 * j + n:4 * j + n + 1] for n in range(4)]
                v(nc.vector.tensor_scalar(y, x, w[3], None, ALU.mult))
                for n in range(3):
                    s = 3 - n
                    v(nc.vector.scalar_tensor_tensor(out=y[:, s:], in0=x[:, 0:T - s], scalar=w[n], in1=y[:, s:],
                                                     op0=ALU.mult, op1=ALU.add), conv if n == 2 else None)

        @block.scalar
        def _(act):
            for j in range(16):
                act.wait_ge(conv, j + 1)
                nc.scalar.activation(qkv[:, j * T:(j + 1) * T], qkv[:, j * T:(j + 1) * T], ACT.Silu).then_inc(act_done, 1)
            for n in range(8):
                act.wait_ge(turned, n + 1)
                b, tt = divmod(n, 2)
                nc.scalar.copy(tok[:, tt * D + b * BANK:tt * D + (b + 1) * BANK], ps[:, n, :]).then_inc(copied, 1)

        @block.tensor
        def _(pe):
            for n in range(8):
                b, tt = divmod(n, 2)
                pe.wait_ge(act_done, 4 * b + 4)
                for j in range(4):
                    c = 4 * b + j
                    mm = nc.tensor.transpose(ps[:, n, j * P:(j + 1) * P], qkv[:, c * T + tt * P:c * T + tt * P + P], k.ident)
                mm.then_inc(turned, 1)


def gdn_gates(k):
    nc, ps = k.nc, k.ps
    tok, qkt, xt = k.at(TOK, 4096), k.at(QKT, 2048), k.at(XT, 2048)
    lm, ltm = k.at(LM, 2048), k.at(LTM, 2048)
    ba, sm = k.at(BA, 32), k.at(GDN_SMALL + 64, 512)
    rows = sm[:, 0:16]
    small = {name: sm[:, 16 + 16 * i:32 + 16 * i] for i, name in enumerate(
        "beta x relu low ex g gc ekd egc bg ss rs root na glast".split())}
    k.gdn = small
    masks = k.at(MASKS, 11 * P)
    (row_in, gsig, soft_in, soft_exp, soft_add, soft_ln, a_exp, ss_in, ss_root, normed, turned, copied, gc_in, gc_sum,
     gc_copied, gb_ready, gr_sum, d_ready, d_exp, e_ready) = (k.sem("gg_" + n) for n in (
         "rows beta low exp one_plus log a_exp squares roots normed turned copied g_ready gc_sum gc_copied g_spread "
         "gc_rows diffs exps small_exp").split())
    th = lambda a: a.rearrange("p (t h) -> p t h", t=TT)
    m3 = lambda a: a.rearrange("p (n s) -> p n s", s=P)
    qk4 = tok.rearrange("p (t c d) -> p t c d", t=TT, d=P)[:, :, 0:8, :]

    with nc.Block() as block:
        @block.sync
        def _(sp):
            sp.dma_start(rows, k.ins["gdn_rows"]).then_inc(row_in, 16)

        @block.scalar
        def _(act):
            a = k.stepper(act, k.astep)
            b3 = th(ba)
            a(nc.scalar.activation(th(small["beta"]), b3[:, :, 0:8], ACT.Sigmoid), gsig)
            act.wait_ge(soft_in, 1)
            a(nc.scalar.activation(small["ex"], small["low"], ACT.Exp), soft_exp)
            act.wait_ge(row_in, 16)
            a(nc.scalar.activation(small["na"][:, 0:8], rows[:, 0:8], ACT.Exp), a_exp)
            act.wait_ge(soft_add, 1)
            a(nc.scalar.activation(small["ex"], small["ex"], ACT.Ln), soft_ln)
            act.wait_ge(ss_in, 1)
            a(nc.scalar.activation(small["root"], small["ss"], ACT.Sqrt), ss_root)
            for n in range(4):
                act.wait_ge(turned, n + 1)
                a(nc.scalar.copy(qkt[:, n * BANK:(n + 1) * BANK], ps[:, n, :]), copied)
            act.wait_ge(d_ready, 1)
            a(nc.scalar.activation(lm, lm, ACT.Exp, scale=-1.0), d_exp)
            act.wait_ge(d_ready, 2)
            a(nc.scalar.activation(ltm, ltm, ACT.Exp), d_exp)
            a(nc.scalar.activation(small["ekd"], small["ekd"], ACT.Exp), e_ready)
            a(nc.scalar.activation(small["egc"], small["gc"], ACT.Exp), e_ready)

        @block.vector
        def _(dve):
            v = k.stepper(dve, k.vstep)
            tt_, ts_ = nc.vector.tensor_tensor, nc.vector.tensor_scalar
            dt = rows[:, 8:16].unsqueeze(1).to_broadcast([P, TT, 8])
            dve.wait_ge(row_in, 16)
            v(tt_(th(small["x"]), th(ba)[:, :, 8:16], dt, ALU.add))
            v(ts_(small["relu"], small["x"], 0.0, None, ALU.max))
            v(ts_(small["low"], small["x"], -1.0, None, ALU.mult))
            v(tt_(small["low"], small["low"], small["x"], ALU.min), soft_in)
            dve.wait_ge(soft_exp, 1)
            v(ts_(small["ex"], small["ex"], 1.0, None, ALU.add), soft_add)
            x4 = xt.rearrange("p (t c d) -> p t c d", t=TT, d=P)
            v(tt_(x4, qk4, qk4, ALU.mult))
            v(nc.vector.tensor_reduce(th(small["ss"]), x4, AX.X, ALU.add))
            dve.wait_ge(soft_ln, 1)
            dve.wait_ge(a_exp, 1)
            v(tt_(small["relu"], small["relu"], small["ex"], ALU.add))
            v(ts_(small["na"][:, 0:8], small["na"][:, 0:8], -1.0, None, ALU.mult))
            v(tt_(th(small["g"]), th(small["relu"]), small["na"][:, 0:8].unsqueeze(1).to_broadcast([P, TT, 8]), ALU.mult),
              gc_in)
            v(ts_(small["ss"], small["ss"], EPS, None, ALU.add), ss_in)
            v(nc.vector.tensor_copy(m3(xt), small["g"].unsqueeze(2).to_broadcast([P, 16, P])), gb_ready)
            dve.wait_ge(ss_root, 1)
            v(nc.vector.reciprocal(small["rs"], small["root"]))
            q_rs = th(small["rs"])[:, :, 0:4]
            v(ts_(q_rs, q_rs, float(BDK) ** -0.5, None, ALU.mult))
            for tt in range(TT):
                v(tt_(qk4[:, tt], qk4[:, tt], small["rs"][:, tt * 8:tt * 8 + 8].unsqueeze(2).to_broadcast([P, 8, P]),
                      ALU.mult), normed)
            dve.wait_ge(gc_sum, 1)
            v(nc.vector.tensor_copy(small["gc"], ps[:, 4, 0:16]), gc_copied)
            dve.wait_ge(gr_sum, 1)
            r3 = ps[:, 4:8, :].rearrange("p b n -> p (b n)").rearrange("p (n s) -> p n s", s=P)
            v(tt_(m3(lm), r3, small["gc"].unsqueeze(2).to_broadcast([P, 16, P]), ALU.subtract))
            v(nc.vector.tensor_copy(small["ekd"].unsqueeze(2), m3(lm)[:, :, P - 1:P]))
            v(ts_(ltm, lm, 0.0, None, ALU.min))
            v(ts_(lm, lm, 0.0, None, ALU.max), d_ready)
            v(ts_(small["bg"], small["gc"], 0.0, None, ALU.add), d_ready)
            dve.wait_ge(e_ready, 2)
            dve.wait_ge(gsig, 1)
            v(tt_(small["bg"], small["beta"], small["egc"], ALU.mult))
            mk = lambda o: masks[:, o:o + P].unsqueeze(1).to_broadcast([P, 16, P])
            dve.wait_ge(d_exp, 2)
            v(tt_(m3(lm), m3(lm), mk(TRIL_S), ALU.mult))
            v(tt_(m3(lm), m3(lm), small["beta"].unsqueeze(2).to_broadcast([P, 16, P]), ALU.mult))
            v(tt_(m3(ltm), m3(ltm), mk(TRIU), ALU.mult))
            for tt in range(TT):
                v4 = tok.rearrange("p (t c d) -> p t c d", t=TT, d=P)[:, tt, 8:16, :]
                v(tt_(v4, v4, small["beta"][:, tt * 8:tt * 8 + 8].unsqueeze(2).to_broadcast([P, 8, P]), ALU.mult))

        @block.tensor
        def _(pe):
            pe.wait_ge(gc_in, 1)
            nc.tensor.matmul(ps[:, 4, 0:16], masks[:, TRIU:TRIU + P], small["g"], start=True, stop=True).then_inc(gc_sum, 1)
            pe.wait_ge(gb_ready, 1)
            pe.wait_ge(gc_copied, 1)
            for n in range(16):
                mm = nc.tensor.matmul(ps[:, 4 + n // 4, (n % 4) * P:(n % 4) * P + P], xt[:, n * P:(n + 1) * P],
                                      masks[:, TRIU:TRIU + P], start=True, stop=True)
            mm.then_inc(gr_sum, 1)
            pe.wait_ge(normed, TT)
            for n in range(4):
                for j in range(2):
                    for tt in range(TT):
                        c = 2 * n + j
                        mm = nc.tensor.transpose(ps[:, n, j * T + tt * P:j * T + tt * P + P],
                                                 tok[:, tt * D + c * P:tt * D + c * P + P], k.ident)
                mm.then_inc(turned, 1)


def gdn_solve(k):
    nc, ps = k.nc, k.ps
    qkt, lm, ltm, nm, aq = k.at(QKT, 2048), k.at(LM, 2048), k.at(LTM, 2048), k.at(NM, 2048), k.at(AQ, 2048)
    tm, um, qm, cm = k.at(TM, 2048), k.at(UM, 2048), k.at(QM, 2048), k.at(CM, 2048)
    levels = k.at(MASKS + LEVELS, 7 * P)
    (kk_sum, n_ready, c_ready, q_sum, q_copied, dt_sum, du_sum, t_done, u_done, first) = (k.sem("gs_" + n) for n in (
        "kk_sum n_ready c_ready q_sum q_copied dt_sum du_sum t_done u_done c0_turned").split())
    half = lambda a, f: a[:, f * 1024:(f + 1) * 1024]
    m3 = lambda a: a.rearrange("p (n s) -> p n s", s=P)
    wide = lambda b: ps[:, b:b + 2, :].rearrange("p b n -> p (b n)")
    NL = 7

    def block_of(b, n):
        return ps[:, b + n // 4, (n % 4) * P:(n % 4) * P + P]

    with nc.Block() as block:
        @block.tensor
        def _(pe):
            for tt in range(TT):
                for h in range(BQH):
                    q_at, k_at = h * T + tt * P, (BQH + h) * T + tt * P
                    mm = nc.tensor.matmul(ps[:, tt, h * P:(h + 1) * P], qkt[:, k_at:k_at + P], qkt[:, k_at:k_at + P],
                                          start=True, stop=True)
                    mm = nc.tensor.matmul(ps[:, 2 + tt, h * P:(h + 1) * P], qkt[:, k_at:k_at + P],
                                          qkt[:, q_at:q_at + P], start=True, stop=True)
                mm.then_inc(kk_sum, 1)
            for f in range(2):
                pe.wait_ge(c_ready, f + 1)
                if f == 0:
                    pe.wait_ge(n_ready, 4)
                for n in range(8):
                    mm = nc.tensor.transpose(block_of(4 * f, n), cm[:, f * 1024 + n * P:f * 1024 + n * P + P], k.ident)
                mm.then_inc(first, 1)
            for lv in range(1, NL):
                for f in range(2):
                    pe.wait_ge(u_done, 2 * (lv - 1) + f + 1)
                    pe.wait_ge(c_ready, 2 * lv + f + 1)
                    for n in range(8):
                        at = f * 1024 + n * P
                        mm = nc.tensor.matmul(block_of(4 * f, n), cm[:, at:at + P], um[:, at:at + P], start=True, stop=True)
                    mm.then_inc(q_sum, 1)
                for f in range(2):
                    pe.wait_ge(q_copied, 2 * (lv - 1) + f + 1)
                    for n in range(8):
                        at = f * 1024 + n * P
                        mm = nc.tensor.matmul(block_of(4 * f + 2, n), qm[:, at:at + P], tm[:, at:at + P], start=True, stop=True)
                    mm.then_inc(dt_sum, 1)
                    for n in range(8):
                        at = f * 1024 + n * P
                        mm = nc.tensor.matmul(block_of(4 * f, n), tm[:, at:at + P], qm[:, at:at + P], start=True, stop=True)
                    mm.then_inc(du_sum, 1)

        @block.scalar
        def _(act):
            for lv in range(1, NL):
                for f in range(2):
                    act.wait_ge(q_sum, 2 * (lv - 1) + f + 1)
                    if lv > 1:
                        act.wait_ge(du_sum, 2 * (lv - 2) + f + 1)
                    nc.scalar.copy(half(qm, f), wide(4 * f)).then_inc(q_copied, 1)

        @block.gpsimd
        def _(pool):
            for lv in range(NL):
                mask = levels[:, lv * P:(lv + 1) * P].unsqueeze(1).to_broadcast([P, 8, P])
                for f in range(2):
                    pool.wait_ge(n_ready, 2 * f + 2)
                    if lv:
                        if lv == 1:
                            pool.wait_ge(first, f + 1)
                            pool.wait_ge(t_done, f + 1)
                        else:
                            pool.wait_ge(q_sum, 2 * (lv - 2) + f + 1)
                    nc.gpsimd.tensor_tensor(m3(half(cm, f)), m3(half(nm, f)), mask, ALU.mult).then_inc(c_ready, 1)

        @block.vector
        def _(dve):
            v = k.stepper(dve, k.vstep)
            tt_ = nc.vector.tensor_tensor
            for f in range(2):
                dve.wait_ge(kk_sum, f + 1)
                for b, dst, m in ((f, nm, lm), (2 + f, aq, ltm)):
                    two = lambda a: half(a, f).rearrange("p (h r s) -> p h r s", h=BQH, r=2)
                    v(tt_(two(dst), ps[:, b, :].rearrange("p (h s) -> p h s", h=BQH).unsqueeze(2).to_broadcast(
                        [P, BQH, 2, P]), two(m), ALU.mult), n_ready)
            eye = k.ident.unsqueeze(1).to_broadcast([P, 8, P])
            for f in range(2):
                dve.wait_ge(c_ready, f + 1)
                v(tt_(m3(half(tm, f)), eye, m3(half(cm, f)), ALU.subtract), t_done)
                dve.wait_ge(first, f + 1)
                v(tt_(m3(half(um, f)), eye, m3(wide(4 * f)), ALU.subtract), u_done)
            for lv in range(1, NL):
                for f in range(2):
                    dve.wait_ge(du_sum, 2 * (lv - 1) + f + 1)
                    v(tt_(half(tm, f), half(tm, f), wide(4 * f + 2), ALU.subtract), t_done)
                    v(tt_(half(um, f), half(um, f), wide(4 * f), ALU.subtract), u_done)


def gdn_outputs(k):
    nc, ps = k.nc, k.ps
    qkt, tok, um, aq, mix, small = k.at(QKT, 2048), k.at(TOK, 4096), k.at(UM, 2048), k.at(AQ, 2048), k.at(MIX, 4096), k.gdn
    kd, vn, state, r, oq = k.at(QM, 1024), k.at(QM + 1024, 1024), k.at(CM, 1024), k.at(CM + 1024, 1024), k.at(NM, 1024)
    (vn_sum, vn_ready, kd_ready, o_sum, s_sum, s_ready, ks_sum, r_ready, qs_sum, o0_out) = (k.sem("go_" + n) for n in (
        "values_sum values kd_ready out_sum state_sum state ks_sum r_ready qs_sum out0_copied").split())
    wide = lambda b: ps[:, b:b + 2, :].rearrange("p b n -> p (b n)")
    h3 = lambda a: a.rearrange("p (h d) -> p h d", h=BVH)
    v_of = lambda tt: tok[:, tt * D + 1024:(tt + 1) * D]
    spread = lambda name, tt: small[name][:, tt * 8:tt * 8 + 8].unsqueeze(2).to_broadcast([P, BVH, P])

    def eight(pe, b, lhs, rhs):
        for h in range(BVH):
            mm = nc.tensor.matmul(ps[:, b + h // 4, (h % 4) * P:(h % 4) * P + P], lhs(h), rhs(h), start=True, stop=True)
        return mm

    head = lambda a, h: a[:, h * P:(h + 1) * P]
    with nc.Block() as block:
        @block.tensor
        def _(pe):
            eight(pe, 0, lambda h: head(um, h), lambda h: head(v_of(0), h)).then_inc(vn_sum, 1)
            pe.wait_ge(vn_ready, 1)
            pe.wait_ge(kd_ready, 1)
            eight(pe, 4, lambda h: head(kd, h), lambda h: head(vn, h)).then_inc(s_sum, 1)
            eight(pe, 2, lambda h: head(aq, h), lambda h: head(vn, h)).then_inc(o_sum, 1)
            pe.wait_ge(s_ready, 1)
            k1 = lambda h: qkt[:, (BQH + h // 2) * T + P:(BQH + h // 2) * T + 2 * P]
            q1 = lambda h: qkt[:, (h // 2) * T + P:(h // 2) * T + 2 * P]
            eight(pe, 6, k1, lambda h: head(state, h)).then_inc(ks_sum, 1)
            eight(pe, 4, q1, lambda h: head(state, h)).then_inc(qs_sum, 1)
            pe.wait_ge(r_ready, 1)
            eight(pe, 0, lambda h: head(um, 8 + h), lambda h: head(r, h)).then_inc(vn_sum, 1)
            pe.wait_ge(vn_ready, 2)
            pe.wait_ge(o0_out, 1)
            eight(pe, 2, lambda h: head(aq, 8 + h), lambda h: head(vn, h)).then_inc(o_sum, 1)

        @block.scalar
        def _(act):
            act.wait_ge(vn_sum, 1)
            nc.scalar.copy(vn, wide(0)).then_inc(vn_ready, 1)
            act.wait_ge(s_sum, 1)
            nc.scalar.copy(state, wide(4)).then_inc(s_ready, 1)
            act.wait_ge(o_sum, 1)
            nc.scalar.copy(mix[:, 1024:2048], wide(2)).then_inc(o0_out, 1)
            act.wait_ge(vn_sum, 2)
            nc.scalar.copy(vn, wide(0)).then_inc(vn_ready, 1)

        @block.vector
        def _(dve):
            v = k.stepper(dve, k.vstep)
            tt_ = nc.vector.tensor_tensor
            kt = tok[:, 512:1024].rearrange("p (h d) -> p h d", h=BQH).unsqueeze(2).to_broadcast([P, BQH, 2, P])
            ek = small["ekd"][:, 0:8].rearrange("p (h r) -> p h r", r=2).unsqueeze(3).to_broadcast([P, BQH, 2, P])
            v(tt_(kd.rearrange("p (h r d) -> p h r d", h=BQH, r=2), kt, ek, ALU.mult), kd_ready)
            dve.wait_ge(ks_sum, 1)
            v(tt_(h3(r), h3(wide(6)), spread("bg", 1), ALU.mult))
            v(tt_(r, v_of(1), r, ALU.subtract), r_ready)
            dve.wait_ge(qs_sum, 1)
            v(tt_(h3(oq), h3(wide(4)), spread("egc", 1), ALU.mult))
            dve.wait_ge(o_sum, 2)
            v(tt_(mix[:, D + 1024:2 * D], oq, wide(2), ALU.add))


def gated_norms(block, k, ready):
    nc = k.nc
    mix, sq, z = k.at(MIX, 4096), k.at(FREE, 4096), k.at(FREE + 4096, 4096)
    gains, st = k.at(FREE + 8192, 256), k.at(FREE + 8448, 160)
    g_in, squared, mean, root, silu = (k.sem("gn_" + n) for n in "gains squared means roots silu".split())
    m4 = mix.rearrange("p (t h d) -> p t h d", t=TT, d=P)

    @block.scalar
    def _(act):
        a = k.stepper(act, k.astep)
        act.dma_start(gains, k.ins["head_norms"]).then_inc(g_in, 16)
        a(nc.scalar.activation(sq, mix, ACT.Square), squared)
        for i, base in enumerate((PR_AG, PR_BZ)):
            for tt in range(TT):
                src = k.at(base, 2048).rearrange("p (w t n) -> p w t n", t=TT, n=256)[:, :, tt, :]
                dst = z[:, tt * D + i * 1024:tt * D + (i + 1) * 1024].rearrange("p (w n) -> p w n", n=256)
                a(nc.scalar.activation(dst, src, ACT.Silu), silu)
        act.wait_ge(mean, 1)
        a(nc.scalar.activation(st[:, 64:96], st[:, 32:64], ACT.Sqrt), root)

    @block.vector
    def _(dve):
        v = k.stepper(dve, k.vstep)
        tt_ = nc.vector.tensor_tensor
        dve.wait_ge(squared, 1)
        v(nc.vector.tensor_reduce(st[:, 0:32], sq.rearrange("p (n d) -> p n d", d=P), AX.X, ALU.add))
        v(nc.vector.tensor_scalar(st[:, 32:64], st[:, 0:32], 1.0 / P, EPS, ALU.mult, ALU.add), mean)
        dve.wait_ge(g_in, 16)
        dve.wait_ge(silu, 4)
        for i in range(2):
            z4 = z.rearrange("p (t h d) -> p t h d", t=TT, d=P)
            for tt in range(TT):
                zz = z4[:, tt, 8 * i:8 * i + 8, :]
                v(tt_(zz, zz, gains[:, i * P:(i + 1) * P].unsqueeze(1).to_broadcast([P, 8, P]), ALU.mult))
        dve.wait_ge(root, 1)
        v(nc.vector.reciprocal(st[:, 96:128], st[:, 64:96]))
        for tt in range(TT):
            v(tt_(m4[:, tt], m4[:, tt], st[:, 96 + 16 * tt:112 + 16 * tt].unsqueeze(2).to_broadcast([P, 16, P]), ALU.mult))
            v(tt_(mix[:, tt * D:(tt + 1) * D], mix[:, tt * D:(tt + 1) * D], z[:, tt * D:(tt + 1) * D], ALU.mult), ready)
    return [(ready, TT)]


H3 = 34816


def second_mixers(k):
    second_inputs(k)
    hgrn(k)
    gdn_convolve(k)
    gdn_gates(k)
    gdn_solve(k)
    gdn_outputs(k)
    mixed = k.sem("mix_ready")
    mixT = k.split_x(MIX_LOW)
    k.transposes(k.at(MIX, 4096), mixT, AT_OUT2, lambda block: gated_norms(block, k, mixed))
    k.project_residual(AT_OUT2, N_OUT2, mixT, k.at(H2, 4096), 1.0, k.at(H3, 4096), AT_WQ)
    return k.at(H3, 4096)


WG, HN_LOW, YACC = 0, 32768, H3
QRY, SUBK, SC, CAND = 8192, 12288, 14336, 18432
TOPS = 22528
E1T, E2T, GT = (RING0 + 2 * PIECE + T * i - WORK0 for i in range(3))
LOWEST = -3.0e38


def sixteen(k, v, values, out, index):
    vector = k.nc.vector
    v(vector.max(out[:, 0:8], values))
    v(vector.max_index(index[:, 0:8], out[:, 0:8], values))
    v(vector.match_replace(values, out[:, 0:8], values, LOWEST))
    v(vector.max(out[:, 8:16], values))
    v(vector.max_index(index[:, 8:16], out[:, 8:16], values))


def peer_queries(k):
    nc, ps = k.nc, k.ps
    normed = k.sem("hn_ready")
    hT = k.split_x(HN_LOW)
    k.transposes(k.at(0, 4096), hT, AT_WQ, lambda block: (
        k.rms_scale(block, k.at(H3, 4096), "ffn_norm_g_2", k.at(4096, 2048), k.at(6144, 16), k.at(0, 4096),
                    "ffn", normed) or [(normed, TT)]))
    qry, subk, sc = k.at(QRY, 4096), k.at(SUBK, 2048), k.at(SC, 4096)
    top, top_i = k.at(TOPS, 512), k.at(TOPS + 512, 512).bitcast(U32)
    keys_in, copied, sums = k.sem("sub_keys"), k.sem("queries_copied"), k.sem("scores_sum")
    with nc.Block() as block:
        @block.sync
        def _(sp):
            sp.dma_start(subk, k.ins["sub_keys"]).then_inc(keys_in, 16)
            k.stream(sp, AT_EXPERTS, ahead=False)

        @block.tensor
        def _(pe):
            def scores(h):
                pe.wait_ge(k.bank_free, AT_WQ + h + 1 + BANKS)
                if h >= 5:
                    pe.wait_ge(copied, h - 4)
                for tt in range(TT):
                    for c in (2 * h, 2 * h + 1):
                        at = tt * 256 + (c % 2) * P
                        mm = nc.tensor.matmul(ps[:, 3 + h % 5, at:at + P], qry[:, c * T + tt * P:c * T + tt * P + P],
                                              subk[:, c * P:(c + 1) * P], start=True, stop=True)
                mm.then_inc(sums, 1)

            pe.wait_ge(keys_in, 16)
            for h in range(PH):
                k.multiply(pe, AT_WQ + h, 1, hT, "channel")
                if h:
                    scores(h - 1)
            scores(PH - 1)

        @block.scalar
        def _(act):
            def copy(h):
                act.wait_ge(sums, h + 1)
                nc.scalar.copy(sc.rearrange("p (t n) -> p t n", t=TT)[:, :, h * 256:(h + 1) * 256],
                               ps[:, 3 + h % 5, :].rearrange("p (t n) -> p t n", t=TT)).then_inc(copied, 1)

            for c in range(PIECES * AT_WQ, PIECES * (AT_WQ + 1)):
                k.high(act, c)
            for h in range(PH):
                if h + 1 < PH:
                    for c in range(PIECES * (AT_WQ + h + 1), PIECES * (AT_WQ + h + 2)):
                        k.high(act, c)
                act.wait_ge(k.multiplied, PIECES * (AT_WQ + h + 1))
                nc.scalar.copy(qry[:, h * BANK:(h + 1) * BANK], ps[:, (AT_WQ + h) % BANKS, :]).then_inc(k.bank_free, 1)
                if h:
                    copy(h - 1)
            copy(PH - 1)

        @block.vector
        def _(dve):
            v = k.stepper(dve, k.vstep)

            def best(h):
                dve.wait_ge(copied, h + 1)
                for tt in range(TT):
                    for r in (tt * 16 + 2 * h, tt * 16 + 2 * h + 1):
                        sixteen(k, v, sc[:, r * P:(r + 1) * P], top[:, r * 16:(r + 1) * 16], top_i[:, r * 16:(r + 1) * 16])

            for h in range(PH):
                for c in range(PIECES * (AT_WQ + h), PIECES * (AT_WQ + h + 1)):
                    k.low(dve, c)
                if h >= 2:
                    best(h - 2)
            best(PH - 2)
            best(PH - 1)


def peer_choose(k):
    nc, ps = k.nc, k.ps
    cand = k.at(CAND, 4096)
    at = lambda i, n=512: k.at(TOPS + 512 * i, n)
    top, top_i, top_f = at(0), at(1).bitcast(U32), at(2)
    best, pos, half_u, e1, e2, gate, pf = (at(3 + i, 256) for i in range(7))
    pos, half_u = pos.bitcast(U32), half_u.bitcast(U32)
    s16 = at(10, 16)
    big = k.at(TOPS + 512 * 11, 4096)
    n_rows = 16
    r3 = lambda a: a.rearrange("p (n j) -> p n j", j=TOPK)
    r4 = lambda a: a.rearrange("p (n i j) -> p n i j", i=TOPK, j=TOPK)
    shape4 = [P, n_rows, TOPK, TOPK]
    raised, e_done, chosen, turned = k.sem("pc_raised"), k.sem("pc_exp"), k.sem("pc_chosen"), k.sem("pc_turned")

    with nc.Block() as block:
        @block.vector
        def _(dve):
            v = k.stepper(dve, k.vstep)
            tt_, ts_ = nc.vector.tensor_tensor, nc.vector.tensor_scalar

            v(nc.vector.tensor_copy(top_f, top_i))
            t4 = top.rearrange("p (n a j) -> p n a j", a=2, j=TOPK)
            f4 = top_f.rearrange("p (n a j) -> p n a j", a=2, j=TOPK)
            v(tt_(r4(cand), t4[:, :, 0, :].unsqueeze(3).to_broadcast(shape4),
                  t4[:, :, 1, :].unsqueeze(2).to_broadcast(shape4), ALU.add))
            for r in range(n_rows):
                sixteen(k, v, cand[:, r * 256:(r + 1) * 256], best[:, r * 16:(r + 1) * 16], pos[:, r * 16:(r + 1) * 16])
            v(tt_(r3(gate), r3(best), r3(best)[:, :, 0:1].to_broadcast([P, n_rows, TOPK]), ALU.subtract), raised)
            for a, (op, by, dst) in enumerate(((ALU.logical_shift_right, 4, e1), (ALU.bitwise_and, 15, e2))):
                v(ts_(half_u, pos, by, None, op))
                v(nc.vector.tensor_copy(pf, half_u))
                v(tt_(r4(big), r3(pf).unsqueeze(3).to_broadcast(shape4),
                      k.iota[:, 0:TOPK].unsqueeze(1).unsqueeze(1).to_broadcast(shape4), ALU.is_equal))
                v(tt_(r4(big), r4(big), f4[:, :, a, :].unsqueeze(2).to_broadcast(shape4), ALU.mult))
                v(nc.vector.tensor_reduce(r3(dst), r4(big), AX.X, ALU.add), chosen)
            dve.wait_ge(e_done, 1)
            v(nc.vector.tensor_reduce(s16, r3(gate), AX.X, ALU.add))
            v(nc.vector.reciprocal(s16, s16))
            v(tt_(r3(gate), r3(gate), s16.unsqueeze(2).to_broadcast([P, n_rows, TOPK]), ALU.mult), chosen)
            for i, dst in enumerate((E1T, E2T, GT)):
                dve.wait_ge(turned, i + 1)
                v(nc.vector.tensor_copy(k.at(dst, T), ps[:, i, 0:T]))

        @block.scalar
        def _(act):
            act.wait_ge(raised, 1)
            nc.scalar.activation(gate, gate, ACT.Exp).then_inc(e_done, 1)

        @block.tensor
        def _(pe):
            for i, src in enumerate((e1, e2, gate)):
                pe.wait_ge(chosen, i + 1)
                for tt in range(TT):
                    mm = nc.tensor.transpose(ps[:, i, tt * P:(tt + 1) * P], src[:, tt * P:(tt + 1) * P], k.ident)
                mm.then_inc(turned, 1)


def peer_gate_matrix(k):
    nc, ps = k.nc, k.ps
    w = k.at(WG, 32768).rearrange("p (i t) -> p t i", t=T)
    e1, e2, gate = (k.at(o, T) for o in (E1T, E2T, GT))
    rows = [k.raw(i)[:, 0:512] for i in range(2)]
    cols = [k.raw(i)[:, 512:] for i in range(2)]
    PER = 4
    rounds = T // PER // 2
    rows_ready, cols_ready, product, placed = (k.sem("gm_" + n) for n in "rows_ready cols_ready product placed".split())

    def twice(eng, body):
        for b in range(2):
            body(b, b, True)
        with eng.Fori(1, rounds) as r:
            for b in range(2):
                body(r * 2 + b, b, False)

    with nc.Block() as block:
        @block.vector
        def _(dve):
            def body(n, b, fresh):
                if not fresh:
                    dve.wait_ge(product, n - 1)
                for j in range(PER):
                    last = nc.vector.tensor_scalar(rows[b][:, j * P:(j + 1) * P], k.iota, e1[:, bass.ds(n * PER + j, 1)],
                                                   gate[:, bass.ds(n * PER + j, 1)], ALU.is_equal, ALU.mult)
                last.then_inc(rows_ready, 1)
                nc.vector.tensor_tensor(cols[b].rearrange("p (j i) -> p j i", i=P),
                                        k.iota.unsqueeze(1).to_broadcast([P, PER, P]),
                                        e2[:, bass.ds(n * PER, PER)].unsqueeze(2).to_broadcast([P, PER, P]),
                                        ALU.is_equal).then_inc(cols_ready, 1)
            twice(dve, body)

        @block.tensor
        def _(pe):
            def body(n, b, fresh):
                pe.wait_ge(rows_ready, n + 1)
                pe.wait_ge(cols_ready, n + 1)
                if not fresh:
                    pe.wait_ge(placed, n - 1)
                for j in range(PER):
                    mm = nc.tensor.matmul(ps[:, b, j * P:(j + 1) * P], rows[b][:, j * P:(j + 1) * P],
                                          cols[b][:, j * P:(j + 1) * P], start=True, stop=True)
                mm.then_inc(product, 1)
            twice(pe, body)

        @block.scalar
        def _(act):
            def body(n, b, fresh):
                act.wait_ge(product, n + 1)
                nc.scalar.copy(w[:, bass.ds(n * PER, PER), :],
                               ps[:, b, :].rearrange("p (j i) -> p j i", i=P)).then_inc(placed, 1)
            twice(act, body)


def peer_experts(k):
    nc, ps = k.nc, k.ps
    x, w, y = k.split_x(HN_LOW), k.at(WG, 32768), k.at(YACC, 4096)
    gparts = [k.split_small(P + 256 * i - WORK0, 512, 512 * i) for i in range(2)]
    gelu_done, gated, g_high, g_low, y_full, y_free = (k.sem("ex_" + n) for n in (
        "gelu_done gated g_high g_low y_full y_free").split())
    BODY = 6
    rounds = (PAIRS - 4) // BODY
    PER = 2 * PIECES * BODY

    def u_piece(j, part, looped=False):
        return PIECES * (AT_EXPERTS + (0 if j == 0 and not looped else 2 * j - 1)) + part

    def v_piece(j, part):
        return PIECES * (AT_EXPERTS + (2 * j + 2 if j < PAIRS - 1 else 2 * PAIRS - 1)) + part

    def run(eng, step):
        for j in range(BODY):
            step(j, 0, False)
        with eng.Fori(1, rounds) as m:
            for j in range(BODY):
                step(j, m, True)
        for j in range(rounds * BODY, PAIRS):
            step(j, 0, False)

    with nc.Block() as block:
        @block.sync
        def _(sp):
            k.stream(sp, N_TILES)

        @block.tensor
        def _(pe):
            def up(j, m, looped):
                if looped or j >= 3:
                    pe.wait_ge(gated, m * BODY + (j - 2))
                for part in range(PIECES):
                    c = u_piece(j, part)
                    pe.wait_ge(k.low_done, m * PER + (c + 1))
                    for half in range(2):
                        for kk in range(KC // PIECES):
                            kc = part * (KC // PIECES) + kk
                            pairs = channel_products(k.parts(c % SLOTS), x,
                                                     slice(kk * 256 + half * P, kk * 256 + half * P + P),
                                                     slice(kc * T, (kc + 1) * T))
                            for i, (a, b) in enumerate(pairs):
                                mm = nc.tensor.matmul(ps[:, j % 3, half * T:half * T + T], a, b,
                                                      start=(kc == 0 and half == 0 and i == 0),
                                                      stop=(kc == KC - 1 and half == 1 and i == 2),
                                                      skip_group_check=True)
                    mm.then_inc(k.multiplied, 1)

            def down(j, m, looped):
                pe.wait_ge(g_low, m * BODY + (j + 1))
                for part in range(PIECES):
                    c = v_piece(j, part)
                    pe.wait_ge(k.low_done, m * PER + (c + 1))
                    for tt in range(TT):
                        n = 8 * j + 2 * part + tt
                        if looped or n >= 4:
                            pe.wait_ge(y_free, m * 8 * BODY + (n - 3))
                        for half in range(2):
                            pairs = token_products(k.parts(c % SLOTS), gparts[j % 2],
                                                   slice(half * BANK, (half + 1) * BANK),
                                                   slice(half * T + tt * P, half * T + tt * P + P))
                            for i, (a, b) in enumerate(pairs):
                                mm = nc.tensor.matmul(ps[:, 4 + n % 4, :], a, b, start=(half == 0 and i == 0),
                                                      stop=(half == 1 and i == 2))
                        mm.then_inc(k.multiplied if tt else y_full, 1)

            def step(j, m, looped):
                if looped or j + 1 < PAIRS:
                    up(j + 1, m, looped)
                down(j, m, looped)

            up(0, 0, False)
            run(pe, step)

        @block.scalar
        def _(act):
            def step(j, m, looped):
                act.wait_ge(k.multiplied, m * PER + (u_piece(j, PIECES - 1, looped) + 1))
                nc.scalar.activation(ps[:, j % 3, :], ps[:, j % 3, :], ACT.Gelu).then_inc(gelu_done, 1)
                act.wait_ge(gated, m * BODY + (j + 1))
                if looped or j >= 2:
                    act.wait_ge(k.multiplied, m * PER + (v_piece(j - 2, PIECES - 1) + 1))
                nc.scalar.copy(gparts[j % 2][0], w[:, bass.ds(m * (512 * BODY) + j * 512, 512)]).then_inc(g_high, 1)
                for part in range(PIECES):
                    k.high(act, v_piece(j, part), m, PER)
                if looped or j + 2 < PAIRS:
                    for part in range(PIECES):
                        k.high(act, u_piece(j + 2, part), m, PER)

            for c in range(PIECES * AT_EXPERTS, PIECES * (AT_EXPERTS + 2)):
                k.high(act, c)
            run(act, step)

        @block.vector
        def _(dve):
            def collect(j, m, looped, part):
                for tt in range(TT):
                    n = 8 * j + 2 * part + tt
                    if tt:
                        dve.wait_ge(k.multiplied, m * PER + (v_piece(j, part) + 1))
                    else:
                        dve.wait_ge(y_full, m * PIECES * BODY + (PIECES * j + part + 1))
                    if looped or n:
                        dve.wait_ge(y_free, m * 8 * BODY + n)
                    a = tt * D + part * BANK
                    nc.vector.tensor_tensor(y[:, a:a + BANK], y[:, a:a + BANK], ps[:, 4 + n % 4, :],
                                            ALU.add).then_inc(y_free, 1)

            def step(j, m, looped):
                high, low = gparts[j % 2]
                gates = w[:, bass.ds(m * (512 * BODY) + j * 512, 512)]
                dve.wait_ge(gelu_done, m * BODY + (j + 1))
                nc.vector.tensor_tensor(gates, ps[:, j % 3, :], gates, ALU.mult).then_inc(gated, 1)
                dve.wait_ge(g_high, m * BODY + (j + 1))
                nc.vector.tensor_tensor(low, gates, high.bitcast(F32), ALU.subtract).then_inc(g_low, 1)
                for part in range(PIECES):
                    k.low(dve, v_piece(j, part), m, PER)
                for part in range(PIECES):
                    if looped or j + 2 < PAIRS:
                        for u in {0: (0, 1), 1: (2,), 2: (3,), 3: ()}[part]:
                            k.low(dve, u_piece(j + 2, u), m, PER)
                    collect(j, m, looped, part)

            for c in range(PIECES * AT_EXPERTS, PIECES * (AT_EXPERTS + 2)):
                k.low(dve, c)
            run(dve, step)
            dve.wait_ge(y_free, 8 * PAIRS)


def final_norm(k):
    nc = k.nc
    normed, stored = k.sem("out_ready"), k.sem("out_stored")
    out = k.at(0, 4096)
    with nc.Block() as block:
        k.rms_scale(block, k.at(YACC, 4096), "final_norm_g_2", k.at(4096, 2048), k.at(6144, 16), out, "final", normed)

        @block.sync
        def _(sp):
            for tt in range(TT):
                sp.wait_ge(normed, tt + 1)
                sp.dma_start(k.out[:, tt * D:(tt + 1) * D], out[:, tt * D:(tt + 1) * D]).then_inc(stored, 16)
            sp.wait_ge(stored, 16 * TT)


def program(k):
    pre = first_block(k)
    k.layer_norm(pre, k.at(H2, 4096), 1, k.at(26624, 2048), k.at(28672, 2048), k.at(30720, 64), None, 0)
    k.new_part()
    second_mixers(k)
    k.new_part()
    peer_queries(k)
    peer_choose(k)
    peer_gate_matrix(k)
    peer_experts(k)
    final_norm(k)


def host_arrays(v):
    f = np.float32
    v = {name: np.asarray(a) for name, a in v.items()}

    def tiles(w, width):
        kk, n = w.shape
        w = w.reshape(PIECES, kk // P // PIECES, P, n // width, width).transpose(3, 0, 2, 1, 4)
        return w.reshape(PIECES * (n // width), P, PIECE)

    def rows(a):
        n, m = a.shape
        return a.reshape(n // P, P, m).transpose(1, 0, 2).reshape(P, -1)

    def spread(a):
        return np.broadcast_to(a, (P, a.shape[-1]))

    def diagonal(a):
        a = a.reshape(STILES, 2, STATE, GCH)
        out = np.zeros((2, STATE, STILES, 2, GCH), f)
        for s in range(2):
            out[s, :, :, s, :] = a[:, s].transpose(1, 0, 2)
        return out.reshape(P, STILES * 32)

    def states(a):
        return a.reshape(STILES, P).T

    x = v["x"][0]
    b_in, w2 = v["b_w_in"][0], v["w_in_2"][0]
    i = np.arange(P)
    q, n = np.arange(T).reshape(TT, P).T[:, :, None], np.arange(16)
    seen = n * CSTRIDE + CBLOCK - 1 <= q
    lower = i[None, :] <= i[:, None]
    weights = [tiles(v["a_w_in"][0], 256), tiles(v["a_w_glu"][0], 512), tiles(v["a_w_out"][0], 512),
               tiles(v["kv_w"], 256), tiles(b_in[:, :8192], 256), tiles(v["b_w_out"][0], 256),
               tiles(w2[:, :7168], 256), tiles(v["w_out_2"][0], 256),
               tiles(v["peer_w_query_2"][0].reshape(D, D), 256)]
    u = v["peer_u_2"][0].reshape(P, PAIRS, 2, PIECES, KC // PIECES, P).transpose(1, 3, 5, 4, 2, 0)
    u = u.reshape(PAIRS, PIECES, P, PIECE)
    vt = v["peer_v_2"][0].reshape(P, PAIRS, 2, PIECES, D // PIECES).transpose(1, 3, 0, 2, 4)
    vt = vt.reshape(PAIRS, PIECES, P, PIECE)
    experts = np.empty((2 * PAIRS, PIECES, P, PIECE), f)
    experts[0] = u[0]
    experts[1:-1:2] = u[1:]
    experts[2:-1:2] = vt[:-1]
    experts[-1] = vt[-1]
    chunk = i[:, None] // CH == i[None, :] // CH
    levels = [(i[:, None] // (2 * m) == i[None, :] // (2 * m)) & (i[:, None] % (2 * m) >= m) & (i[None, :] % (2 * m) < m)
              for m in (1, 2, 4, 8, 16, 32, 64)]
    arrays = {
        "x_t": rows(np.ascontiguousarray(x.T)), "x_rows": rows(x),
        "weights": np.concatenate(weights), "experts": experts.reshape(2 * PAIRS * PIECES, P, PIECE),
        "consts": np.concatenate([np.eye(P, dtype=f), spread(np.arange(P))], 1),
        "s5_states": np.concatenate([states(v["a_lam_re"][0]), states(v["a_lam_im"][0]),
                                     states(np.repeat(v["a_log_dt"][0][:, None], STATE, 1))], 1),
        "s5_b_re": diagonal(v["a_b_re"][0]), "s5_b_im": diagonal(v["a_b_im"][0]),
        "s5_c_re": diagonal(v["a_c_re"][0].transpose(0, 2, 1)), "s5_c_im": diagonal(v["a_c_im"][0].transpose(0, 2, 1)),
        "s5_channels": np.concatenate([v["a_d"][0].reshape(ECH, P).T, v["a_b_glu"][0].reshape(ECH, P).T], 1),
        "cmp_w1_k": rows(v["cmp_w1_k"]), "cmp_w1_v": rows(v["cmp_w1_v"]),
        "cmp_w2_k": v["cmp_w2_k"], "cmp_w2_v": v["cmp_w2_v"],
        "cmp_pos_k": v["cmp_pos_k"].T, "cmp_pos_v": v["cmp_pos_v"].T,
        "w_gate": rows(b_in[:, 8192:]),
        "ln_g": np.stack([spread(v["ln_g"][n]) for n in range(2)]),
        "ln_b": np.stack([spread(v["ln_b"][n]) for n in range(2)]),
        "att_masks": np.concatenate([np.where(lower, 0.0, NEG), np.where(seen, 0.0, NEG).reshape(P, -1),
                                     seen.reshape(P, -1)], 1),
        "attn_norm_g_2": spread(v["attn_norm_g_2"][0]), "ffn_norm_g_2": spread(v["ffn_norm_g_2"][0]),
        "final_norm_g_2": spread(v["final_norm_g_2"]),
        "w_beta": rows(w2[:, 7168:]),
        "hgrn_lb": v["hgrn_lb_logits_2"].transpose(2, 0, 1).reshape(P, -1),
        "head_norms": np.concatenate([spread(v["hgrn_norm_g_2"][0]), spread(v["gdn_norm_g_2"][0])], 1),
        "conv_w": v["gdn_conv_w_2"][0].reshape(4, 16, P).transpose(2, 1, 0).reshape(P, 64),
        "gdn_rows": np.concatenate([spread(v["gdn_A_log_2"][0]), spread(v["gdn_dt_bias_2"][0])], 1),
        "masks2": np.concatenate([lower.T, lower.T & ~np.eye(P, dtype=bool), lower, lower & ~np.eye(P, dtype=bool),
                                  (lower.T & chunk).reshape(P, NCH, CH).sum(1)] + levels, 1),
        "sub_keys": v["peer_sub_keys_2"][0].transpose(3, 1, 0, 2).reshape(P, -1),
    }
    return {name: np.ascontiguousarray(a, dtype=f) for name, a in arrays.items()}


def build(nc, shapes):
    ins = {name: nc.dram_tensor(name, shape, F32, kind="ExternalInput").ap() for name, shape in shapes.items()}
    out = nc.dram_tensor("out", (P, TT * D), F32, kind="ExternalOutput").ap()
    with ExitStack() as ctx:
        program(Kernel(nc, ctx, ins, out))


def kernel(**inputs):
    import concourse.bacc as bacc
    from concourse.bass_utils import run_bass_kernel_spmd

    nc = bacc.Bacc("TRN2", target_bir_lowering=False, num_devices=1, dynamic_dma_scratch_size=1024)
    arrays = host_arrays(inputs)
    build(nc, {name: a.shape for name, a in arrays.items()})
    got = run_bass_kernel_spmd(nc, [arrays], core_ids=[0]).results[0]["out"]
    return np.asarray(got).reshape(P, TT, D).transpose(1, 0, 2).reshape(1, T, D)
```
